# Optimizing a Trainium2 kernel written in Bass

```python
import jax, jax.numpy as jnp
from jax import lax
import numpy as np

D_MODEL = 1024
BATCH = 1
SEQ = 256
DEPTH = 1
DEC_BATCH = 1
DEC_SEQ = 64
PAST_LEN = 128

CHUNK = 64
A_HEADS = 8
A_DK = 128
A_DV = 128
D_A = A_HEADS * A_DK
D_B = D_MODEL // 2
CONV_K = 31
N_EXPERTS = 16
N_GROUPS = 4
EXP_PER_GROUP = N_EXPERTS // N_GROUPS
TOP_K = 2
D_FF = D_MODEL
MASK_SCORE = -1.0e4
N_IN = 4 * D_A + 2 * D_B + 2 * D_MODEL
SPLITS = [D_A, 2 * D_A, 3 * D_A, 4 * D_A, 4 * D_A + D_B, 4 * D_A + 2 * D_B,
          4 * D_A + 2 * D_B + D_MODEL]
DN_ALPHA = (2 * DEPTH) ** 0.25
DN_BETA = (8 * DEPTH) ** -0.25
LN_EPS = 1e-5

kernel_name = "hgrn2_conformer_gated_moe_stream_step"

def layer_norm(x, g, b):
    xf = x.astype(jnp.float32)
    mu = jnp.mean(xf, -1, keepdims=True)
    var = jnp.mean(jnp.square(xf - mu), -1, keepdims=True)
    return ((xf - mu) * lax.rsqrt(var + LN_EPS) * g + b).astype(x.dtype)

def rms_norm(x, g):
    xf = x.astype(jnp.float32)
    return xf * lax.rsqrt(jnp.mean(xf * xf, -1, keepdims=True) + LN_EPS) * g

def hgrn_lower_bounds(lb_logits):
    p = jax.nn.softmax(lb_logits.astype(jnp.float32), axis=0)
    return jnp.cumsum(p, axis=0) - p[0]

def gla_block(S, q, k, v, logf):
    L = q.shape[2]
    b = jnp.cumsum(logf, axis=2)
    causal = jnp.tril(jnp.ones((L, L), dtype=jnp.float32))[None, None, :, :, None]
    diff = b[:, :, :, None, :] - b[:, :, None, :, :]
    decay = jnp.exp(jnp.minimum(diff, 0.0)) * causal
    attn = jnp.einsum('bhtd,bhsd,bhtsd->bhts', q, k, decay)
    o = (jnp.einsum('bhts,bhsv->bhtv', attn, v)
         + jnp.einsum('bhtd,bhdv->bhtv', q * jnp.exp(b), S))
    b_last = b[:, :, -1:, :]
    k_dec = k * jnp.exp(b_last - b)
    S_new = (jnp.exp(b_last[:, :, 0, :])[..., None] * S
             + jnp.einsum('bhsd,bhsv->bhdv', k_dec, v))
    return S_new, o

def hgrn_scan(S0, q, k, v, logf):
    B, H, T, _ = q.shape
    n = T // CHUNK

    def to_blocks(a):
        return a.reshape(B, H, n, CHUNK, a.shape[-1]).transpose(2, 0, 1, 3, 4)

    def step(S, blk):
        return gla_block(S, *blk)

    S, o = lax.scan(step, S0, (to_blocks(q), to_blocks(k), to_blocks(v), to_blocks(logf)))
    o = o.transpose(1, 2, 0, 3, 4).reshape(B, H, T, -1)
    return S, o

def token_mixer(h, hg_state, conv_hist, lb, blocked, w_in, hg_norm_g, w_o_a,
                conv_w, conv_b, cn_g, cn_b, w_o_b, w_out):
    B, T, _ = h.shape
    f32 = jnp.float32
    proj = jnp.einsum('btd,dn->btn', h, w_in)
    q, f_pre, i_v, g_o, u_a, u_b, gate_a, gate_b = jnp.split(proj, SPLITS, axis=-1)

    zf = f_pre.astype(f32)
    lb = lb.astype(f32)
    logf = jax.nn.log_sigmoid(zf) + jnp.log1p(lb * jnp.exp(-zf))
    k = (1.0 - lb) * jax.nn.sigmoid(-zf)

    def heads(a):
        return a.astype(f32).reshape(B, T, A_HEADS, -1).transpose(0, 2, 1, 3)

    qh = heads(q) * (A_DK ** -0.5)
    kh, vh, lfh = heads(k), heads(i_v), heads(logf)
    S0 = hg_state.astype(f32)
    if blocked:
        S_new, o = hgrn_scan(S0, qh, kh, vh, lfh)
    else:
        S_new, o = gla_block(S0, qh, kh, vh, lfh)
    o = rms_norm(o, hg_norm_g).transpose(0, 2, 1, 3).reshape(B, T, D_A).astype(h.dtype)
    o = o * jax.nn.silu(g_o)
    y_a = jnp.einsum('btc,cd->btd', o, w_o_a)

    u = u_a * jax.nn.sigmoid(u_b)
    u_full = jnp.concatenate([conv_hist.astype(u.dtype), u], axis=1)
    c = lax.conv_general_dilated(
        u_full, conv_w[:, None, :].astype(u.dtype), window_strides=(1,), padding='VALID',
        dimension_numbers=('NWC', 'WIO', 'NWC'), feature_group_count=D_B) + conv_b
    c = jax.nn.silu(layer_norm(c, cn_g, cn_b))
    y_b = jnp.einsum('btc,cd->btd', c, w_o_b)
    new_conv = u_full[:, -(CONV_K - 1):, :]

    m = jax.nn.sigmoid(gate_a) * y_a + jax.nn.sigmoid(gate_b) * y_b
    out = jnp.einsum('btd,de->bte', m, w_out)
    return out, S_new, new_conv

def moe(h, w_router, router_bias, w_gate, w_up, w_down):
    B, T, _ = h.shape
    f32 = jnp.float32
    logits = jnp.einsum('btd,de->bte', h, w_router).astype(f32)
    scores = jax.nn.softmax(logits, axis=-1)
    sel = scores + router_bias.astype(f32)
    sel_g = sel.reshape(B, T, N_GROUPS, EXP_PER_GROUP)
    group_score = lax.top_k(sel_g, TOP_K)[0].sum(-1)
    g_idx = jnp.argmax(group_score, axis=-1)
    group_mask = jax.nn.one_hot(g_idx, N_GROUPS, dtype=jnp.bool_)[..., None]
    masked = jnp.where(group_mask, sel_g, MASK_SCORE).reshape(B, T, N_EXPERTS)
    _, e_idx = lax.top_k(masked, TOP_K)
    w_sel = jnp.take_along_axis(scores, e_idx, axis=-1)
    w_sel = w_sel / jnp.sum(w_sel, -1, keepdims=True)
    gates = jnp.sum(jax.nn.one_hot(e_idx, N_EXPERTS, dtype=f32) * w_sel[..., None], axis=-2)
    gates = gates.astype(h.dtype)
    y = jnp.zeros_like(h)
    for e in range(N_EXPERTS):
        a = jnp.einsum('btd,df->btf', h, w_gate[e])
        u = jnp.einsum('btd,df->btf', h, w_up[e])
        y = y + gates[..., e:e + 1] * jnp.einsum('btf,fd->btd', jax.nn.silu(a) * u, w_down[e])
    return y

def trunk(x, hg_state, conv_state, blocked, p):
    (ln_in_g, ln_in_b, w_in, lb_logits, hg_norm_g, w_o_a, conv_w, conv_b, cn_g, cn_b,
     w_o_b, w_out, ln1_g, ln1_b, w_router, router_bias, w_gate_e, w_up_e, w_down_e,
     ln2_g, ln2_b) = p
    lbs = hgrn_lower_bounds(lb_logits)
    x = layer_norm(x, ln_in_g, ln_in_b)
    new_hg, new_conv = [], []
    for l in range(DEPTH):
        mix, S_l, c_l = token_mixer(x, hg_state[l], conv_state[l], lbs[l], blocked,
                                    w_in[l], hg_norm_g[l], w_o_a[l], conv_w[l], conv_b[l],
                                    cn_g[l], cn_b[l], w_o_b[l], w_out[l])
        x = layer_norm(DN_ALPHA * x + mix, ln1_g[l], ln1_b[l])
        ff = moe(x, w_router, router_bias, w_gate_e[l], w_up_e[l], w_down_e[l])
        x = layer_norm(DN_ALPHA * x + ff, ln2_g[l], ln2_b[l])
        new_hg.append(S_l.astype(x.dtype))
        new_conv.append(c_l.astype(x.dtype))
    return x, jnp.stack(new_hg), jnp.stack(new_conv)

def setup_inputs(seed: int = 0) -> dict:
    key = jax.random.key(seed)
    ks = jax.random.split(key, 32)
    n = lambda i, s: jax.random.normal(ks[i], s, jnp.float32)
    return {
        "x_prompt": n(0, (BATCH, SEQ, D_MODEL)),
        "x_sample": n(1, (DEC_BATCH, DEC_SEQ, D_MODEL)),
        "state_hgrn": 0.3 * n(2, (DEPTH, DEC_BATCH, A_HEADS, A_DK, A_DV)),
        "state_conv": 0.5 * n(3, (DEPTH, DEC_BATCH, CONV_K - 1, D_B)),
        "ln_in_g": 1.0 + 0.05 * n(4, (D_MODEL,)),
        "ln_in_b": 0.05 * n(5, (D_MODEL,)),
        "w_in": n(6, (DEPTH, D_MODEL, N_IN)) * D_MODEL ** -0.5,
        "lb_logits": 0.5 * n(7, (DEPTH, D_A)),
        "hg_norm_g": 1.0 + 0.05 * n(8, (DEPTH, A_DV)),
        "w_o_a": n(9, (DEPTH, D_A, D_MODEL)) * (D_A ** -0.5 * DN_BETA),
        "conv_w": n(10, (DEPTH, CONV_K, D_B)) * CONV_K ** -0.5,
        "conv_b": 0.02 * n(11, (DEPTH, D_B)),
        "cn_g": 1.0 + 0.05 * n(12, (DEPTH, D_B)),
        "cn_b": 0.05 * n(13, (DEPTH, D_B)),
        "w_o_b": n(14, (DEPTH, D_B, D_MODEL)) * (D_B ** -0.5 * DN_BETA),
        "w_out": n(15, (DEPTH, D_MODEL, D_MODEL)) * (D_MODEL ** -0.5 * DN_BETA),
        "ln1_g": 1.0 + 0.05 * n(16, (DEPTH, D_MODEL)),
        "ln1_b": 0.05 * n(17, (DEPTH, D_MODEL)),
        "w_router": n(18, (D_MODEL, N_EXPERTS)) * D_MODEL ** -0.5,
        "router_bias": 0.01 * n(19, (N_EXPERTS,)),
        "w_gate_e": n(20, (DEPTH, N_EXPERTS, D_MODEL, D_FF)) * D_MODEL ** -0.5,
        "w_up_e": n(21, (DEPTH, N_EXPERTS, D_MODEL, D_FF)) * D_MODEL ** -0.5,
        "w_down_e": n(22, (DEPTH, N_EXPERTS, D_FF, D_MODEL)) * (D_FF ** -0.5 * DN_BETA),
        "ln2_g": 1.0 + 0.05 * n(23, (DEPTH, D_MODEL)),
        "ln2_b": 0.05 * n(24, (DEPTH, D_MODEL)),
    }

def reference(x_prompt, x_sample, state_hgrn, state_conv, ln_in_g, ln_in_b, w_in, lb_logits,
              hg_norm_g, w_o_a, conv_w, conv_b, cn_g, cn_b, w_o_b, w_out, ln1_g, ln1_b,
              w_router, router_bias, w_gate_e, w_up_e, w_down_e, ln2_g, ln2_b):
    p = (ln_in_g, ln_in_b, w_in, lb_logits, hg_norm_g, w_o_a, conv_w, conv_b, cn_g, cn_b,
         w_o_b, w_out, ln1_g, ln1_b, w_router, router_bias, w_gate_e, w_up_e, w_down_e,
         ln2_g, ln2_b)
    bp = x_prompt.shape[0]
    hg0 = jnp.zeros((DEPTH, bp, A_HEADS, A_DK, A_DV), x_prompt.dtype)
    cv0 = jnp.zeros((DEPTH, bp, CONV_K - 1, D_B), x_prompt.dtype)
    y_prompt, hg_prompt, conv_prompt = trunk(x_prompt, hg0, cv0, True, p)
    y_sample, hg_sample, conv_sample = trunk(x_sample, state_hgrn, state_conv, False, p)
    return (y_prompt, y_sample, hg_prompt, conv_prompt, hg_sample, conv_sample)


_drawn_inputs = setup_inputs


def setup_inputs(seed=0):
    import zlib

    import numpy as np

    out = dict(_drawn_inputs(seed))
    spreads = {}
    factors = {'state_hgrn': 6.875, 'hg_norm_g': 4.051, 'conv_b': 4.279, 'cn_g': 4.054, 'cn_b': 3.331}
    for name, (base, spread) in spreads.items():
        noise = np.random.default_rng([zlib.crc32(name.encode()), seed]).standard_normal(out[name].shape)
        drawn = base * np.exp(spread * noise) if base else spread * noise
        out[name] = __import__('jax').numpy.asarray(drawn.astype(out[name].dtype))
    for name, factor in factors.items():
        out[name] = (out[name] * factor).astype(out[name].dtype)
    return out
```

```python
from contextlib import ExitStack

import concourse.bass as bass
from concourse import mybir

F32 = mybir.dt.float32
BF16 = mybir.dt.bfloat16
I32 = mybir.dt.int32
ALU = mybir.AluOpType
ACT = mybir.ActivationFunctionType
AX_X = mybir.AxisListType.X

P = 128
D = 1024
KT = D // P
SEQ, DEC = 256, 64
T = SEQ + DEC
HEADS = 8
DB = 512
CT = DB // P
TAPS = 31
HALO = TAPS - 1
UW = HALO + SEQ + HALO + DEC
CW = UW - HALO
NE = 16
GR = 4
CAP = 64
PAIRS = NE // 2
ROUNDS = T // CAP
RING = 4
EPS = 1e-5
ALPHA = 2.0 ** 0.25
QSCALE = float(P) ** -0.5
MASK_SCORE = -1.0e4
TILES = [(0, 128), (128, 128), (256, 64)]
LV = [64, 32, 16, 8, 4, 2, 1]
XO = [0] + [256 + i * T for i in range(6)]
XW = 256 + 6 * T
COFF = {"ident": 0, "reset": 128, "tri": 128 + T, "i64": 256 + T, "i16": 320 + T, "i4": 336 + T}
CWID = 340 + T
Q0, F0, V0, G0, UA0, UB0, GA0, GB0 = 0, D, 2 * D, 3 * D, 4 * D, 4 * D + DB, 5 * D, 6 * D


def shape_constants():
    import numpy as np

    c = np.zeros((P, CWID), np.float32)
    c[:, 0:P] = np.eye(P)
    c[:, COFF["reset"]:COFF["reset"] + T] = 1.0
    for t0, _ in TILES:
        c[:, COFF["reset"] + t0] = 0.0
    c[:, COFF["tri"]:COFF["tri"] + P] = np.triu(np.ones((P, P)), 1)
    c[:, COFF["i64"]:COFF["i64"] + CAP] = np.arange(CAP)
    c[:, COFF["i16"]:COFF["i16"] + NE] = np.arange(NE)
    c[:, COFF["i4"]:COFF["i4"] + GR] = np.arange(GR)
    s, t = np.arange(P)[:, None], np.arange(P)[None, :]
    m = [(s // (2 * h) == t // (2 * h)) & (s % (2 * h) < h) & (t % (2 * h) >= h) for h in LV]
    m.append(s == t)
    return c, np.stack(m, 1).reshape(P, 8 * P).astype(np.float32)


X0_BANKS = [0, 1, 2, 3, 0, 1]
X1_BANKS = [6, 7, 0, 1, 2, 3]
U_BANKS = [(0, 1), (2, 3), (5, 7), (0, 1)]


class Chain:

    def __init__(self, eng, sem, per=0):
        self.eng, self.sem, self.per, self.base, self.n = eng, sem, per, 0, 0

    def turn(self, i):
        self.base, self.n = (i * self.per if self.per else 0), 0

    def __call__(self, ins):
        self.n += 1
        ins.then_inc(self.sem, 1)
        self.eng.wait_ge(self.sem, self.base + self.n)

    def end(self):
        assert self.n == self.per, (self.n, self.per)


def signal(eng, ins, sem, value):
    ins.then_inc(sem, 1)
    eng.wait_ge(sem, value)


def build(nc, a, o):
    with ExitStack() as ctx:
        def sb(name, shape, dt=F32):
            return ctx.enter_context(nc.sbuf_tensor(name, shape, dt))

        def sem(name):
            return ctx.enter_context(nc.semaphore(name))

        ring = sb("ring", [P, RING, 2, 4, D])
        slots = ring[:, RING - 1].rearrange("p b k n -> p b (k n)")
        cst = sb("cst", [P, CWID])
        ones_t = sb("ones", [P, P])
        ones = ones_t[:, :]
        xT = sb("xT", [P, KT, T])
        mid = sb("mid", [P, KT * T + CT * CW + 4 * P])
        oT = mid[:, 0:KT * T].rearrange("p (k n) -> p k n", k=KT)
        cT = mid[:, KT * T:KT * T + CT * CW].rearrange("p (c n) -> p c n", c=CT)
        mask = mid[:, KT * T + CT * CW:].bitcast(BF16).rearrange("p (l n) -> p l n", l=8)
        vt = sb("vt", [P, CT, 64])
        hv = sb("hv", [P, 9])
        lb = sb("lb", [P, 8])
        olb = sb("olb", [P, 8])
        utail = sb("utail", [P, CT, 2, HALO])
        stats = sb("stats", [P, 3, 2, 6])
        mv = sb("mv", [P, 3, 2])
        rstd3 = sb("rstd3", [P, 3])
        one1 = sb("one1", [P, 1])
        eps1 = sb("eps1", [P, 1])
        AR = 11950
        ar = sb("ar", [P, AR])
        ps = ctx.enter_context(nc.psum_tensor("ps", [P, 8, 512], F32))

        def carve(first, *sizes):
            out, at = [], first
            for n in sizes:
                out.append(ar[:, at:at + n])
                at += n
            assert at <= AR, at
            return out

        ident = cst[:, 0:P]
        reset = cst[:, COFF["reset"]:COFF["reset"] + T]
        tri = cst[:, COFF["tri"]:COFF["tri"] + P]
        i64 = cst[:, COFF["i64"]:COFF["i64"] + CAP]
        i16 = cst[:, COFF["i16"]:COFF["i16"] + NE]
        i4 = cst[:, COFF["i4"]:COFF["i4"] + GR]

        x0f, gb0, rows_a, hrows_a, maskf = carve(0, 3 * D, 2 * D, DB, P, 8 * P)
        x0 = x0f.rearrange("p (t n) -> p t n", t=3)
        gb0 = gb0.rearrange("p (g n) -> p g n", g=2)
        ucf, sgu_f, acc, alI = carve(9100, CT * UW, 2 * T, CW, P)
        uc = ucf.rearrange("p (b n) -> p b n", b=CT)
        sgu = sgu_f.rearrange("p (b n) -> p b n", b=2)
        (hq, hk, hsg, hV, he, hw, hls, hb, hgx, heb, hqeb, hkde, hkT, hAM0, hAM1, hAS, hSA, hSst, hSo, hosq, hrs, hebl) = carve(
            0, 2 * T, 2 * T, 2 * T, 384, T, T, T, T, T, T, T, T, 384, 1024, 1024, 384, P, 2 * P, 2 * P, T, T, 4)
        two = lambda v: v.rearrange("p (b n) -> p b n", b=2)
        hq, hk, hsg, hSst, hSo, hebl = two(hq), two(hk), two(hsg), two(hSst), two(hSo), two(hebl)
        hV, hkT, hAS = (v.rearrange("p (b n) -> p b n", b=3) for v in (hV, hkT, hAS))
        hAM = [v.rearrange("p (l n) -> p l n", l=8) for v in (hAM0, hAM1)]
        X = [ring[:, 0, b].rearrange("p k n -> p (k n)")[:, 0:XW] for b in range(2)]
        mTf, sgbf, sgtf, t12f, cnf, csq = carve(0, KT * T, KT * T, 2 * T, 2 * T, CT * T, CT * CW)
        gb1f, ncv = carve(7680, 2 * D, 2 * DB)
        crs = acc
        mT = mTf.rearrange("p (k n) -> p k n", k=KT)
        sgb = sgbf.rearrange("p (k n) -> p k n", k=KT)
        sgt = sgtf.rearrange("p (b n) -> p b n", b=2)
        t12 = t12f.rearrange("p (b n) -> p b n", b=2)
        cn = cnf.rearrange("p (c n) -> p c n", c=CT)
        csq = csq.rearrange("p (c n) -> p c n", c=CT)
        ncv = ncv.rearrange("p (s n) -> p s n", s=2)
        gb1 = gb1f.rearrange("p (g n) -> p g n", g=2)
        x1 = mid[:, 0:3 * D].rearrange("p (t n) -> p t n", t=3)
        g2 = mid[:, 3 * D:4 * D]
        x1T = xT
        b2, yaccf, wrt, rb, L16, S16, Z16, M16, N16, O1, O2, GT16, PS6, G3, G4, rt, cur, cnt, cnti, eXT, ehs, eh, ehT, eos, ePm, eGm, eGT = carve(
            0, D, 3 * D, KT * NE, NE, *[48] * 8, 72, 24, 24, 144, 18, 20, 4, KT * P, D, D, KT * P, D, 384, 384, 384)
        yacc = yaccf.rearrange("p (t n) -> p t n", t=3)
        eXT, ehT = (v.rearrange("p (k n) -> p k n", k=KT) for v in (eXT, ehT))
        ePm, eGm, eGT = (v.rearrange("p (t n) -> p t n", t=3) for v in (ePm, eGm, eGT))
        wrt = wrt.rearrange("p (k n) -> p k n", k=KT)
        L16, S16, Z16, M16, N16, O1, O2, GT16 = (v.rearrange("p (t n) -> p t n", t=3) for v in (L16, S16, Z16, M16, N16, O1, O2, GT16))
        PS6 = PS6.rearrange("p (m s) -> p m s", s=6)
        G3 = G3.rearrange("p (t g) -> p t g", t=6)
        G4 = G4.rearrange("p (t g) -> p t g", t=6)
        rt = rt.rearrange("p (w t n) -> p w t n", w=3, t=3)
        cur = cur.rearrange("p (w t e) -> p w t e", w=3, t=3)
        flag = cnti[:, 0:1].bitcast(I32)

        const_in, mask_in, rows_in, hrows_in, gb0_in = (sem(n) for n in ("const_in", "mask_in", "rows_in", "hrows_in", "gb0_in"))
        x_in = [sem(f"x_in{t}") for t in range(3)]
        setup_done, dve_step, act_step = sem("setup_done"), sem("dve_step"), sem("act_step")
        var0, rstd0, x0_ready, x0T_done, x0T_sb = (sem(n) for n in ("var0", "rstd0", "x0_ready", "x0T_done", "x0T_sb"))
        rowsT_done, params_ready = sem("rowsT_done"), sem("params_ready")
        wu_in = [sem(f"wu_in{c}") for c in range(CT)]
        u_done, sgu_ready, u_ready, conv_done, conv_step = (sem(n) for n in ("u_done", "sgu_ready", "u_ready", "conv_done", "conv_step"))
        wb_in = sem("wb_in")
        yb_done, mb_ready, mb_step = sem("yb_done"), sem("mb_ready"), sem("mb_step")
        wh_in = [sem(f"wh_in{b}") for b in range(2)]
        st_in = [sem(f"st_in{b}") for b in range(2)]
        names = ("f_done q_done g_done v_done e_ready ls_ready w_ready k_ready b_ready dr_ready dl_ready kexp_ready E_ready q_sb gc_ready gx_ready sg_ready "
                 "eb_ready kde_ready xr_ready xl_ready a_done am_ready as_ready qeb_ready kdec_ready kT_done kT_sb s_done sa_sb o_done "
                 "osq_ready rms_done rstd_ready rstd_exp o_out so_ready so_stored hc_dve hp_dve hc_act hp_act hc_pool hp_pool ho_dve v_sb round")
        h = {n: sem(n) for n in names.split()}
        tailT_done, tail_sb, tail_stored = sem("tailT_done"), sem("tail_sb"), sem("tail_stored")
        cmean_done, cdiff_ready, csq_ready, cvar_done, crs_ready, cz_ready, cn_ready = (
            sem(n) for n in ("cmean_done", "cdiff_ready", "csq_ready", "cvar_done", "crs_ready", "cz_ready", "cn_ready"))
        wt_in = [sem(f"wt_in{b}") for b in range(2)]
        t_done, sgt_ready, m_ready, m_step = (sem(n) for n in ("t_done", "sgt_ready", "m_ready", "m_step"))
        wo_in = sem("wo_in")
        gb1_in, gb2_in, wrt_in, rb_in = (sem(n) for n in ("gb1_in", "gb2_in", "wrt_in", "rb_in"))
        mix_done, var1, rstd1, x1_ready, x1T_done, x1T_sb = (sem(n) for n in ("mix_done", "var1", "rstd1", "x1_ready", "x1T_done", "x1T_sb"))
        yacc_ready = sem("yacc_ready")
        logit_done, route_step, lmax_ready, lexp_ready, chosen, pos_done, routed = (
            sem(n) for n in ("logit_done", "route_step", "lmax_ready", "lexp_ready", "chosen", "pos_done", "routed"))
        group_in = [sem(f"group_in{g}") for g in range(RING)]
        names = ("group_used pick_ready gpick_ready eXT_done eXT_a eXT_b eGT_done eGT_sb gate_done up_done silu_ready eh_ready ehT_done ehT_a ehT_b "
                 "down_done eos_ready y_done y_added e_dve e_act")
        e = {n: sem(n) for n in names.split()}
        var2, rstd2, y_ready, y_stored, norm_step, norm_act = (sem(n) for n in ("var2", "rstd2", "y_ready", "y_stored", "norm_step", "norm_act"))

        w_in, w_oa, w_ob, w_out = a["w_in"][0], a["w_o_a"][0], a["w_o_b"][0], a["w_out"][0]
        w_in_k = w_in.rearrange("(k p) n -> p k n", p=P)
        w_oa_k = w_oa.rearrange("(k p) n -> p k n", p=P)
        w_ob_k = w_ob.rearrange("(k p) n -> p k n", p=P)
        w_out_k = w_out.rearrange("(k p) n -> p k n", p=P)
        su = ring[:, 1].rearrange("p b k n -> p (b k n)").rearrange("p (c s k n) -> p c s k n", c=CT, s=2, k=KT)
        sh = slots[:, :, :].rearrange("p b (s k n) -> p b s k n", s=4, k=KT)
        sob = ring[:, 2, 0]
        stl = slots[:, :, 0:24 * P].rearrange("p b (k n) -> p b k n", n=P)
        so = ring[:, 1].rearrange("p b k n -> p (b k) n")
        xp = a["x_prompt"][0].rearrange("(t p) n -> t p n", p=P)
        xs = a["x_sample"][0]

        block = ctx.enter_context(nc.Block())

        def bcast(v, n):
            return v.rearrange("(o n) -> o n", o=1).to_broadcast([P, n])

        @block.sync
        def _(sp):
            sp.dma_start(x0[:, 0, :], xp[0]).then_inc(x_in[0], 16)
            sp.dma_start(x0[:, 1, :], xp[1]).then_inc(x_in[1], 16)
            sp.dma_start(x0[0:DEC, 2, :], xs).then_inc(x_in[2], 16)
            sp.dma_start(cst[:, :], a["consts"]).then_inc(const_in, 16)
            sp.dma_start(gb0[:, 0, :], bcast(a["ln_in_g"], D)).then_inc(gb0_in, 16)
            sp.dma_start(gb0[:, 1, :], bcast(a["ln_in_b"], D)).then_inc(gb0_in, 16)
            sp.dma_start(rows_a[0:TAPS, :], a["conv_w"][0]).then_inc(rows_in, 16)
            sp.dma_start(rows_a[31:32, :], a["conv_b"]).then_inc(rows_in, 16)
            sp.dma_start(rows_a[32:33, :], a["cn_g"]).then_inc(rows_in, 16)
            sp.dma_start(rows_a[33:34, :], a["cn_b"]).then_inc(rows_in, 16)
            sp.dma_start(rows_a[34:64, :], a["state_conv"][0, 0]).then_inc(rows_in, 16)
            sp.dma_start(hrows_a[0:8, :], a["lb_logits"].rearrange("o (h n) -> (o h) n", h=8)).then_inc(hrows_in, 16)
            sp.dma_start(hrows_a[8:9, :], a["hg_norm_g"]).then_inc(hrows_in, 16)
            sp.dma_start(maskf, a["masks"]).then_inc(mask_in, 16)

            def cols(first, c):
                return w_in_k[:, :, bass.ds(first + c * P, P)]

            def load_u(c):
                sp.dma_start(su[:, c, 0], cols(UA0, c)).then_inc(wu_in[c], 16)
                sp.dma_start(su[:, c, 1], cols(UB0, c)).then_inc(wu_in[c], 16)

            def load_head(i, b):
                c = 2 * i + b
                for s, first in enumerate((F0, Q0, G0, V0)):
                    sp.dma_start(sh[:, b, s], cols(first, c)).then_inc(wh_in[b], 16)

            def load_state(i, b):
                sp.dma_start(hSst[:, b, :], a["state_hgrn"][0, 0, bass.ds(2 * i + b, 1)].rearrange("o p n -> (o p) n")).then_inc(st_in[b], 16)

            def load_tail(i, b):
                c = 2 * i + b
                sp.dma_start(stl[:, b, 0:8], cols(GA0, c)).then_inc(wt_in[b], 16)
                sp.dma_start(stl[:, b, 8:16], cols(GB0, c)).then_inc(wt_in[b], 16)
                sp.dma_start(stl[:, b, 16:24], w_oa_k[:, :, bass.ds(c * P, P)]).then_inc(wt_in[b], 16)

            for b in range(2):
                load_head(0, b)
            sp.wait_ge(x0T_done, 6)
            for b in range(2):
                load_state(0, b)
            for c in range(CT):
                load_u(c)
            sp.dma_start(sob, w_ob_k).then_inc(wb_in, 16)
            with sp.Fori(1, 4) as i:
                for b in range(2):
                    sp.wait_ge(h["v_done"], 2 * i + b - 1)
                    load_head(i, b)
                    sp.wait_ge(h["so_ready"], 2 * i + b - 1)
                    sp.wait_ge(h["o_done"], 2 * i + b - 1)
                    load_state(i, b)
            for b in range(2):
                sp.wait_ge(h["v_done"], 7 + b)
                load_tail(0, b)
            with sp.Fori(1, 4) as i:
                for b in range(2):
                    sp.wait_ge(t_done, 2 * i + b - 1)
                    load_tail(i, b)
            sp.dma_start(so, w_out_k).then_inc(wo_in, 16)
            sp.wait_ge(cvar_done, 1)
            sp.dma_start(gb1[:, 0, :], bcast(a["ln1_g"][0], D)).then_inc(gb1_in, 16)
            sp.dma_start(gb1[:, 1, :], bcast(a["ln1_b"][0], D)).then_inc(gb1_in, 16)
            sp.wait_ge(cn_ready, 8)
            sp.dma_start(g2, bcast(a["ln2_g"][0], D)).then_inc(gb2_in, 16)

            wg, wu, wd = (a[n][0].rearrange("e (s k p) n -> s p e k n", p=P, s=2) for n in ("w_gate_e", "w_up_e", "w_down_e"))

            def load_group(i, g):
                src = (wg, wu, wd)[g % 6 // 2][g % 2]
                for m in range(2):
                    sp.dma_start(ring[:, g % RING, m], src[:, bass.ds(4 * i + 2 * (g // 6) + m, 1)].rearrange("p o k n -> p (o k) n")).then_inc(group_in[g % RING], 16)

            load_group(0, 0)
            sp.wait_ge(t_done, 8)
            load_group(0, 3)
            sp.wait_ge(yb_done, 8)
            load_group(0, 2)
            sp.wait_ge(mb_ready, 8)
            sp.dma_start(wrt, a["w_router"].rearrange("(k p) n -> p k n", p=P)).then_inc(wrt_in, 16)
            sp.dma_start(rb, bcast(a["router_bias"], NE)).then_inc(rb_in, 16)
            sp.wait_ge(mix_done, 3)
            load_group(0, 1)
            sp.dma_start(b2, bcast(a["ln2_b"][0], D)).then_inc(gb2_in, 16)
            for g in range(RING, 12):
                sp.wait_ge(e["group_used"], g - RING + 1)
                load_group(0, g)
            with sp.Fori(1, PAIRS // 2) as i:
                for g in range(12):
                    sp.wait_ge(e["group_used"], 12 * i + g - RING + 1)
                    load_group(i, g)
            sp.wait_ge(routed, 1)
            more = sp.value_load(flag[0:1, :], min_val=0, max_val=1)
            with sp.If(more != 0):
                with sp.Fori(1, ROUNDS) as r:
                    with sp.Fori(0, PAIRS // 2) as i:
                        for g in range(12):
                            sp.wait_ge(e["group_used"], 6 * PAIRS * r + 12 * i + g - RING + 1)
                            load_group(i, g)

        @block.tensor
        def _(pe):
            def mm(out, lhsT, rhs, start, stop):
                return pe.matmul(out, lhsT, rhs, start=start, stop=stop)

            pe.wait_ge(const_in, 16)
            pe.wait_ge(rows_in, 80)
            pe.wait_ge(hrows_in, 32)
            pe.wait_ge(setup_done, 1)
            for c in range(CT):
                pe.transpose(ps[:, 7, c * 64:c * 64 + 64], rows_a[0:64, c * P:c * P + P], ident[0:64, 0:64])
            pe.transpose(ps[:, 7, 256:265], hrows_a[0:9, :], ident[0:9, 0:9]).then_inc(rowsT_done, 1)

            def to_features(src, ready, done, copied, banks):
                for t, (_, n) in enumerate(TILES):
                    pe.wait_ge(ready, t + 1)
                    for hf in range(2):
                        bank = banks[2 * t + hf]
                        if bank in banks[:2 * t + hf]:
                            pe.wait_ge(copied, banks.index(bank) + 1)
                        for k in range(4):
                            last = pe.transpose(ps[:, bank, k * P:k * P + n], src[0:n, t, (4 * hf + k) * P:(4 * hf + k + 1) * P], ident[0:n, 0:n])
                        last.then_inc(done, 1)

            to_features(x0, x0_ready, x0T_done, x0T_sb, X0_BANKS)

            def project(bank, w):
                for k in range(KT):
                    last = mm(ps[:, bank, 0:T], w[:, k, :], xT[:, k, :], k == 0, k == KT - 1)
                return last

            pe.wait_ge(x0T_sb, 6)

            def cur_f(i, b, first):
                pe.wait_ge(wh_in[b], i * 64 + 64)
                if not first:
                    pe.wait_ge(h["ls_ready"], 2 * i + b)
                project(0, sh[:, b, 0]).then_inc(h["f_done"], 1)

            def cur_q(i, b, first):
                if not first:
                    pe.wait_ge(h["q_sb"], 2 * i + b)
                project(1, sh[:, b, 1]).then_inc(h["q_done"], 1)

            def cur_g(i, b, first, after_rms):
                if not first:
                    pe.wait_ge(h["sg_ready"], 2 * i + b)
                if after_rms:
                    pe.wait_ge(h["rstd_ready"], 2 * i + b - 1)
                project(2, sh[:, b, 2]).then_inc(h["g_done"], 1)

            def cur_v(i, b, first):
                if not first:
                    pe.wait_ge(h["v_sb"], 2 * i + b)
                for t, (t0, n) in enumerate(TILES):
                    for k in range(KT):
                        last = mm(ps[0:n, 3, t * P:t * P + P], xT[:, k, t0:t0 + n], sh[:, b, 3, k, :], k == 0, k == KT - 1)
                last.then_inc(h["v_done"], 1)

            def levels(i, b, t, first):
                t0, n = TILES[t]
                if t == 0:
                    pe.wait_ge(h["xr_ready"], 2 * i + b + 1)
                    pe.wait_ge(h["xl_ready"], 2 * i + b + 1)
                if not (first and t == 0):
                    pe.wait_ge(h["am_ready"], 3 * (2 * i + b) + t)
                for lv in range(8):
                    if t == 2 and lv == 0:
                        continue
                    lo = ro = None
                    if lv < 7:
                        at = XO[lv] + t0
                        lo = ro = X[b][:, at:at + n]
                    else:
                        lo, ro = hk[:, b, t0:t0 + n], hq[:, b, t0:t0 + n]
                    last = mm(ps[0:n, 4 + lv // 4, (lv % 4) * P:(lv % 4) * P + n], lo, ro, True, True)
                last.then_inc(h["a_done"], 1)

            def prev_kT(i, b, first):
                pe.wait_ge(h["kdec_ready"], 2 * i + b + 1)
                if not first:
                    pe.wait_ge(h["so_ready"], 2 * i + b)
                for t, (t0, n) in enumerate(TILES):
                    last = pe.transpose(ps[0:n, 7, t * P:t * P + P], hkde[:, t0:t0 + n], ident)
                last.then_inc(h["kT_done"], 1)

            def prev_states(i, b):
                n1 = 2 * i + b
                pe.wait_ge(h["kT_sb"], n1 + 1)
                pe.wait_ge(h["v_sb"], n1 + 1)
                for t, (t0, n) in enumerate(TILES):
                    last = mm(ps[:, 7, t * P:t * P + P], hkT[0:n, t, :], hV[0:n, t, :], True, True)
                last.then_inc(h["s_done"], 1)

            def prev_out(i, b, first):
                n1 = 2 * i + b
                if not first:
                    pe.wait_ge(h["o_out"], n1)
                pe.wait_ge(st_in[b], i * 16 + 16)
                pe.wait_ge(h["qeb_ready"], n1 + 1)
                pe.wait_ge(h["sa_sb"], n1 + 1)
                pe.wait_ge(h["as_ready"], 3 * n1 + 2)
                mm(ps[:, 6, 0:128], hV[:, 0, :], hAS[:, 0, :], True, True)
                mm(ps[:, 6, 128:256], hSA, hqeb[:, 128:256], True, False)
                mm(ps[:, 6, 128:256], hV[:, 1, :], hAS[:, 1, :], False, True)
                mm(ps[:, 6, 256:320], hSst[:, b, :], hqeb[:, 256:320], True, False)
                pe.wait_ge(h["as_ready"], 3 * n1 + 3)
                mm(ps[:, 6, 256:320], hV[0:64, 2, :], hAS[0:64, 2, 0:64], False, True).then_inc(h["o_done"], 1)

            def rms(i, b):
                n1 = 2 * i + b
                pe.wait_ge(h["sg_ready"], n1 + 2)
                pe.wait_ge(h["osq_ready"], n1 + 1)
                mm(ps[:, 2, 0:T], ones, hosq, True, True).then_inc(h["rms_done"], 1)

            def head_turn(cur, prev, pprev, first=False, first_prev=False):
                if cur:
                    cur_f(*cur, first)
                if pprev:
                    rms(*pprev)
                if prev:
                    levels(*prev, 0, first_prev)
                if cur:
                    cur_q(*cur, first)
                if prev:
                    levels(*prev, 1, first_prev)
                    prev_kT(*prev, first_prev)
                if cur:
                    cur_g(*cur, first, pprev is not None)
                if prev:
                    levels(*prev, 2, first_prev)
                    prev_states(*prev)
                if cur:
                    cur_v(*cur, first)
                if prev:
                    prev_out(*prev, first_prev)

            head_turn((0, 0), None, None, first=True)
            head_turn((0, 1), (0, 0), None, first_prev=True)
            with pe.Fori(1, 4) as i:
                head_turn((i, 0), (i - 1, 1), (i - 1, 0))
                head_turn((i, 1), (i, 0), (i - 1, 1))

            def conv_value(c):
                pe.wait_ge(wu_in[c], 32)
                project(U_BANKS[c][0], su[:, c, 0])

            def conv_gate(c):
                project(U_BANKS[c][1], su[:, c, 1]).then_inc(u_done, 1)

            rms(3, 0)
            levels(3, 1, 0, False)
            levels(3, 1, 1, False)
            prev_kT(3, 1, False)
            levels(3, 1, 2, False)
            prev_states(3, 1)
            pe.wait_ge(h["rstd_ready"], 7)
            pe.wait_ge(h["sg_ready"], 8)
            pe.wait_ge(h["v_sb"], 8)
            conv_value(0)
            prev_out(3, 1, False)
            conv_gate(0)
            pe.wait_ge(h["osq_ready"], 8)
            pe.wait_ge(h["am_ready"], 24)
            mm(ps[:, 4, 0:T], ones, hosq, True, True).then_inc(h["rms_done"], 1)
            conv_value(1)
            conv_gate(1)
            pe.wait_ge(h["so_ready"], 8)
            conv_value(2)
            conv_gate(2)
            pe.wait_ge(u_ready, 1)
            conv_value(3)
            conv_gate(3)
            pe.wait_ge(h["o_out"], 8)

            def tail(i, b, first):
                pe.wait_ge(wt_in[b], i * 48 + 48)
                if not first:
                    pe.wait_ge(m_ready, 2 * i + b - 1)
                for s, src in enumerate((xT, xT, oT)):
                    for k in range(KT):
                        last = mm(ps[:, 3 * b + s, 0:T], stl[:, b, 8 * s + k, :], src[:, k, :], k == 0, k == KT - 1)
                last.then_inc(t_done, 1)

            pe.wait_ge(u_ready, 4)
            tail(0, 0, True)
            tail(0, 1, True)
            with pe.Fori(1, 3) as i:
                tail(i, 0, False)
                tail(i, 1, False)

            pe.wait_ge(conv_done, 4)
            for c in range(CT):
                last = mm(ps[:, 6, 0:CW], ones, cT[:, c, :], c == 0, c == CT - 1)
            last.then_inc(cmean_done, 1)
            tail(3, 0, False)
            pe.wait_ge(csq_ready, 1)
            for c in range(CT):
                last = mm(ps[:, 7, 0:CW], ones, csq[:, c, :], c == 0, c == CT - 1)
            last.then_inc(cvar_done, 1)
            tail(3, 1, False)
            pe.wait_ge(crs_ready, 1)
            for s in range(2):
                for c in range(CT):
                    last = pe.transpose(ps[0:HALO, 6 + s, c * P:c * P + P], utail[:, c, s, :], ident)
            last.then_inc(tailT_done, 1)
            pe.wait_ge(m_ready, 7)
            pe.wait_ge(cn_ready, 8)
            pe.wait_ge(wb_in, 16)
            for d in range(KT):
                if d == 2:
                    pe.wait_ge(m_ready, 8)
                if d >= 4:
                    pe.wait_ge(mb_ready, d - 3)
                for k in range(CT):
                    last = mm(ps[:, (1, 2, 4, 5)[d % 4], 0:T], sob[:, k, d * P:d * P + P], cn[:, k, :], k == 0, k == CT - 1)
                last.then_inc(yb_done, 1)

            pe.wait_ge(mb_ready, 8)
            pe.wait_ge(wo_in, 16)
            for b in range(2):
                for t, (t0, n) in enumerate(TILES):
                    for k in range(4 * b, 4 * b + 4):
                        for hf in range(2):
                            last = mm(ps[0:n, 2 * t + hf, :], mT[:, k, t0:t0 + n], so[:, k, hf * 512:hf * 512 + 512], k == 0, k == KT - 1)
                        if k == 0:
                            for kk in range(KT):
                                mm(ps[0:n, 2 * t + kk // 4, (kk % 4) * P:(kk % 4) * P + P], xT[:, kk, t0:t0 + n], alI, False, False)
                    if b == 1:
                        last.then_inc(mix_done, 1)

            to_features(x1, x1_ready, x1T_done, x1T_sb, X1_BANKS)
            pe.wait_ge(x1T_sb, 6)
            pe.wait_ge(wrt_in, 16)
            for t, (t0, n) in enumerate(TILES):
                for k in range(KT):
                    last = mm(ps[0:n, 4, t * NE:t * NE + NE], x1T[:, k, t0:t0 + n], wrt[:, k, :], k == 0, k == KT - 1)
            last.then_inc(logit_done, 1)
            pe.wait_ge(chosen, 1)
            for t in range(3):
                for s in range(t + 1):
                    last = mm(ps[:, 5, t * NE:t * NE + NE], tri if s == t else ones, rt[:, 1, s, :], s == 0, s == t)
            for s in range(3):
                last = mm(ps[:, 5, 3 * NE:4 * NE], ones, rt[:, 1, s, :], s == 0, s == 2)
            last.then_inc(pos_done, 1)

            def both(bank, lhs, g):
                for kk in range(4):
                    k = 4 * (g % 2) + kk
                    for hf in range(2):
                        for m in range(2):
                            last = mm(ps[64 * m:64 * m + 64, bank + hf, :], lhs[:, k, 64 * m:64 * m + 64], ring[:, g % RING, m, kk, hf * 512:hf * 512 + 512],
                                      k == 0, k == KT - 1)
                return last

            def group(g, i):
                pe.wait_ge(group_in[g % RING], 32 * (12 // RING) * i + 32 * (g // RING) + 32)

            def expert_pair(i, b, first):
                n = 2 * i + b
                pe.wait_ge(e["pick_ready"], n + 1)
                if not first:
                    pe.wait_ge(e["y_added"], 6 * n)
                for k in range(KT):
                    for t, (_, c) in enumerate(TILES):
                        last = mm(ps[:, 4 + k // 4, (k % 4) * P:(k % 4) * P + P], x1[0:c, t, k * P:k * P + P], ePm[0:c, t, :], t == 0, t == 2)
                last.then_inc(e["eXT_done"], 1)
                pe.wait_ge(e["gpick_ready"], n + 1)
                for t, (_, c) in enumerate(TILES):
                    last = pe.transpose(ps[:, 6, t * P:t * P + c], eGm[0:c, t, :], ident[0:c, 0:c])
                last.then_inc(e["eGT_done"], 1)
                pe.wait_ge(e["eXT_a"], n + 1)
                pe.wait_ge(e["eXT_b"], n + 1)
                for g in range(6 * b, 6 * b + 4):
                    group(g, i)
                    both(0 if g < 6 * b + 2 else 2, eXT, g).then_inc(e["group_used"], 1)
                pe.wait_ge(e["eh_ready"], n + 1)
                for k in range(KT):
                    last = pe.transpose(ps[:, 4 + k // 4, (k % 4) * P:(k % 4) * P + P], eh[:, k * P:k * P + P], ident)
                last.then_inc(e["ehT_done"], 1)
                pe.wait_ge(e["ehT_a"], n + 1)
                pe.wait_ge(e["ehT_b"], n + 1)
                pe.wait_ge(e["eGT_sb"], n + 1)
                for g in range(6 * b + 4, 6 * b + 6):
                    group(g, i)
                    both(6, ehT, g).then_inc(e["group_used"], 1)
                pe.wait_ge(e["eos_ready"], n + 1)
                for t, (_, c) in enumerate(TILES):
                    for hf in range(2):
                        j = 2 * t + hf
                        if j >= 4:
                            pe.wait_ge(e["y_added"], 6 * n + j - 3)
                        mm(ps[0:c, 2 + j % 4, :], eGT[:, t, 0:c], eos[:, hf * 512:hf * 512 + 512], True, True).then_inc(e["y_done"], 1)

            expert_pair(0, 0, True)
            expert_pair(0, 1, False)
            with pe.Fori(1, PAIRS // 2) as i:
                expert_pair(i, 0, False)
                expert_pair(i, 1, False)
            more = pe.value_load(flag[0:1, :], min_val=0, max_val=1)
            with pe.If(more != 0):
                with pe.Fori(1, ROUNDS) as r:
                    with pe.Fori(0, PAIRS // 2) as i:
                        expert_pair(PAIRS // 2 * r + i, 0, False)
                        expert_pair(PAIRS // 2 * r + i, 1, False)

        @block.scalar
        def _(act):
            step = Chain(act, act_step)
            act.preload_act_table_set("natural_log_exp_and_others")
            act.wait_ge(setup_done, 1)

            def rstd_of(var, ready, ch):
                for t in range(3):
                    act.wait_ge(var, t + 1)
                    ch(act.activation(rstd3[:, t:t + 1], mv[:, t, 1:2], ACT.Ln, bias=eps1[:, :]))
                    signal(act, act.activation(rstd3[:, t:t + 1], rstd3[:, t:t + 1], ACT.Exp, scale=-0.5), ready, t + 1)

            rstd_of(var0, rstd0, step)

            def copy_features(dst, done, copied, banks):
                for t, (t0, n) in enumerate(TILES):
                    for hf in range(2):
                        act.wait_ge(done, 2 * t + hf + 1)
                        src = ps[:, banks[2 * t + hf], :].rearrange("p (k n) -> p k n", k=4)[:, :, 0:n]
                        signal(act, act.activation(dst[:, 4 * hf:4 * hf + 4, t0:t0 + n], src, ACT.Copy), copied, 2 * t + hf + 1)

            copy_features(xT, x0T_done, x0T_sb, X0_BANKS)

            cc = Chain(act, h["hc_act"], 6)
            pc = Chain(act, h["hp_act"], 1)
            act.wait_ge(params_ready, 1)

            def forget(i, b, first):
                n = 2 * i + b
                cc.turn(n)
                act.wait_ge(h["f_done"], n + 1)
                if not (first and b == 0):
                    act.wait_ge(h["ls_ready"], n)
                cc(act.activation(he, ps[:, 0, 0:T], ACT.Abs))
                if not (first and b == 0):
                    act.wait_ge(h["b_ready"], n)
                cc(act.activation(hw, ps[:, 0, 0:T], ACT.Exp, scale=-1.0))
                cc(act.activation(he, he, ACT.Exp, scale=-1.0))
                signal(act, act.activation(he, he, ACT.Ln, bias=one1[:, :]), h["e_ready"], n + 1)
                signal(act, act.activation(hw, hw, ACT.Ln, scale=lb[:, bass.ds(n, 1)], bias=one1[:, :]), h["w_ready"], n + 1)

            def q_copy(i, b, first):
                n = 2 * i + b
                act.wait_ge(h["q_done"], n + 1)
                if not first:
                    act.wait_ge(h["a_done"], 3 * n - 3)
                    act.wait_ge(h["qeb_ready"], n - 1)
                signal(act, act.activation(hq[:, b, :], ps[:, 1, 0:T], ACT.Copy, scale=QSCALE), h["q_sb"], n + 1)

            def key_exp(i, b):
                n = 2 * i + b
                act.wait_ge(h["ls_ready"], n + 1)
                signal(act, act.activation(hk[:, b, :], hk[:, b, :], ACT.Exp), h["kexp_ready"], n + 1)

            def g_exp(i, b):
                n = 2 * i + b
                act.wait_ge(h["gc_ready"], n + 1)
                cc(act.activation(hgx, hgx, ACT.Exp, scale=-1.0))
                cc(act.activation(hgx, hgx, ACT.Ln, bias=one1[:, :]))
                signal(act, act.activation(hgx, hgx, ACT.Exp, scale=-1.0), h["gx_ready"], n + 1)

            def v_copy(i, b, first):
                n = 2 * i + b
                act.wait_ge(h["v_done"], n + 1)
                if not first:
                    act.wait_ge(h["o_done"], n)
                cc(act.activation(hV[:, 0:2, :], ps[:, 3, 0:256].rearrange("p (t n) -> p t n", t=2), ACT.Copy))
                signal(act, act.activation(hV[0:64, 2, :], ps[0:64, 3, 256:384], ACT.Copy), h["v_sb"], n + 1)

            def level_exp(i, b):
                n = 2 * i + b
                act.wait_ge(h["dr_ready"], n + 1)
                act.wait_ge(h["dl_ready"], n + 1)
                signal(act, act.activation(X[b], X[b], ACT.Exp), h["E_ready"], n + 1)

            def tile_exp(i, b, first):
                n = 2 * i + b
                if not first:
                    act.wait_ge(h["qeb_ready"], n)
                    act.wait_ge(h["kT_done"], n)
                signal(act, act.activation(heb, hb, ACT.Exp), h["eb_ready"], n + 1)
                for t, (t0, c) in enumerate(TILES):
                    last = act.activation(hkde[:, t0:t0 + c], hb[:, t0:t0 + c], ACT.Exp, scale=-1.0, bias=hb[:, t0 + c - 1:t0 + c])
                    signal(act, last, h["kde_ready"], 3 * n + t + 1)

            def prev_states(i, b, first):
                n = 2 * i + b
                act.wait_ge(h["kT_done"], n + 1)
                if not first:
                    act.wait_ge(h["s_done"], n)
                pc.turn(n)
                pc(act.activation(hkT[:, 0:2, :], ps[:, 7, 0:256].rearrange("p (t n) -> p t n", t=2), ACT.Copy))
                signal(act, act.activation(hkT[0:64, 2, :], ps[0:64, 7, 256:384], ACT.Copy), h["kT_sb"], n + 1)

            def prev_sa(i, b, first):
                n = 2 * i + b
                act.wait_ge(h["s_done"], n + 1)
                if not first:
                    act.wait_ge(h["so_ready"], n)
                    act.wait_ge(h["o_done"], n)
                signal(act, act.activation(hSA, ps[:, 7, 0:P], ACT.Copy), h["sa_sb"], n + 1)

            def prev_square(i, b, first):
                n = 2 * i + b
                act.wait_ge(h["o_done"], n + 1)
                if not first:
                    act.wait_ge(h["rms_done"], n)
                signal(act, act.activation(hosq, ps[:, 6, 0:T], ACT.Square), h["osq_ready"], n + 1)

            def store_states(i, b):
                n = 2 * i + b
                act.wait_ge(h["so_ready"], n + 1)
                for s, name in enumerate(("new_hgrn_prompt", "new_hgrn_sample")):
                    act.dma_start(o[name][0, 0, bass.ds(n, 1)].rearrange("o p n -> (o p) n"), hSo[:, s, :]).then_inc(h["so_stored"], 16)

            def pprev_rms(i, b, first, bank=2):
                n = 2 * i + b
                act.wait_ge(h["rms_done"], n + 1)
                if not first:
                    act.wait_ge(h["o_out"], n)
                signal(act, act.activation(hrs, ps[:, bank, 0:T], ACT.Ln, bias=eps1[:, :], scale=1.0 / P), h["rstd_ready"], n + 1)
                signal(act, act.activation(hrs, hrs, ACT.Exp, scale=-0.5), h["rstd_exp"], n + 1)

            def head_turn(cur, prev, pprev, first=False, first_prev=False, first_pprev=False):
                if cur:
                    forget(*cur, first or first_prev)
                if pprev:
                    pprev_rms(*pprev, first_pprev)
                if cur:
                    key_exp(*cur)
                    q_copy(*cur, first or first_prev)
                if prev:
                    prev_states(*prev, first_prev)
                if cur:
                    level_exp(*cur)
                    tile_exp(*cur, first)
                    g_exp(*cur)
                if prev:
                    prev_sa(*prev, first_prev)
                    prev_square(*prev, first_prev)
                    store_states(*prev)
                if cur:
                    v_copy(*cur, first)

            head_turn((0, 0), None, None, first=True)
            head_turn((0, 1), (0, 0), None, first_prev=True)
            head_turn((1, 0), (0, 1), (0, 0), first_pprev=True)
            head_turn((1, 1), (1, 0), (0, 1))
            with act.Fori(2, 4) as i:
                head_turn((i, 0), (i - 1, 1), (i - 1, 0))
                head_turn((i, 1), (i, 0), (i - 1, 1))
            pprev_rms(3, 0, False)
            prev_states(3, 1, False)
            prev_sa(3, 1, False)

            def conv_gate(i, b):
                n = 2 * i + b
                act.wait_ge(u_done, n + 1)
                if i:
                    act.wait_ge(u_ready, b + 1)
                signal(act, act.activation(sgu[:, b, :], ps[:, U_BANKS[n][1], 0:T], ACT.Sigmoid), sgu_ready, n + 1)

            prev_square(3, 1, False)
            store_states(3, 1)
            conv_gate(0, 0)
            pprev_rms(3, 1, False, bank=4)
            conv_gate(0, 1)
            conv_gate(1, 0)
            conv_gate(1, 1)

            def tail(i, b, first=False):
                n = 2 * i + b
                act.wait_ge(t_done, n + 1)
                if not first:
                    act.wait_ge(m_ready, n - 1)
                signal(act, act.activation(sgt[:, b, :], ps[:, 3 * b, 0:T], ACT.Sigmoid), sgt_ready, 2 * n + 1)
                dst = sgb[:, bass.ds(n, 1), :].rearrange("p o n -> p (o n)")
                signal(act, act.activation(dst, ps[:, 3 * b + 1, 0:T], ACT.Sigmoid), sgt_ready, 2 * n + 2)

            tail(0, 0, True)
            tail(0, 1, True)
            with act.Fori(1, 3) as i:
                tail(i, 0)
                tail(i, 1)

            act.wait_ge(cdiff_ready, 1)
            act.wait_ge(h["so_stored"], 256)
            signal(act, act.activation(csq, cT, ACT.Square), csq_ready, 1)
            tail(3, 0)
            act.wait_ge(cvar_done, 1)
            step(act.activation(crs, ps[:, 7, 0:CW], ACT.Ln, bias=eps1[:, :], scale=1.0 / DB))
            signal(act, act.activation(crs, crs, ACT.Exp, scale=-0.5), crs_ready, 1)
            act.wait_ge(cz_ready, 1)
            for c in range(CT):
                for s, (dst, src) in enumerate(((slice(0, SEQ), slice(0, SEQ)), (slice(SEQ, T), slice(SEQ + HALO, CW)))):
                    signal(act, act.activation(cn[:, c, dst], cT[:, c, src], ACT.Silu, scale=vt[:, c, 32:33], bias=vt[:, c, 33:34]), cn_ready, 2 * c + s + 1)
            tail(3, 1)
            act.wait_ge(tailT_done, 1)
            for s in range(2):
                signal(act, act.activation(ncv[0:HALO, s, :], ps[0:HALO, 6 + s, :], ACT.Copy), tail_sb, s + 1)
                act.dma_start(o[("new_conv_prompt", "new_conv_sample")[s]][0, 0], ncv[0:HALO, s, :]).then_inc(tail_stored, 16)
            act.preload_act_table_set("natural_log_exp_and_others")

            rstd_of(var1, rstd1, step)
            copy_features(x1T, x1T_done, x1T_sb, X1_BANKS)
            act.wait_ge(lmax_ready, 1)
            signal(act, act.activation(L16, L16, ACT.Exp), lexp_ready, 1)
            act.wait_ge(x1_ready, 3)
            for t, (_, n) in enumerate(TILES):
                signal(act, act.activation(yacc[0:n, t, :], x1[0:n, t, :], ACT.Copy, scale=ALPHA), yacc_ready, t + 1)

            def expert_pair(n, first):
                act.wait_ge(e["eXT_done"], n + 1)
                signal(act, act.activation(eXT[:, 0:4, :], ps[:, 4, :].rearrange("p (k n) -> p k n", k=4), ACT.Copy), e["eXT_a"], n + 1)
                act.wait_ge(e["eGT_done"], n + 1)
                signal(act, act.activation(eGT[:, :, :].rearrange("p t n -> p (t n)")[:, 0:T], ps[:, 6, 0:T], ACT.Copy), e["eGT_sb"], n + 1)
                act.wait_ge(e["group_used"], 6 * n + 2)
                signal(act, act.activation(ehs, ps[:, 0:2, :].rearrange("p b n -> p (b n)"), ACT.Silu), e["silu_ready"], n + 1)
                act.wait_ge(e["ehT_done"], n + 1)
                signal(act, act.activation(ehT[:, 0:4, :], ps[:, 4, :].rearrange("p (k n) -> p k n", k=4), ACT.Copy), e["ehT_a"], n + 1)
                act.wait_ge(e["group_used"], 6 * n + 6)
                signal(act, act.activation(eos, ps[:, 6:8, :].rearrange("p b n -> p (b n)"), ACT.Copy), e["eos_ready"], n + 1)

            with act.Fori(0, PAIRS) as p:
                expert_pair(p, False)
            more = act.value_load(flag[0:1, :], min_val=0, max_val=1)
            with act.If(more != 0):
                with act.Fori(1, ROUNDS) as r:
                    with act.Fori(0, PAIRS) as p:
                        expert_pair(PAIRS * r + p, False)
            rstd_of(var2, rstd2, step)
            act.wait_ge(tail_stored, 32)
            act.wait_ge(h["so_stored"], 256)
            for t, (t0, c) in enumerate(TILES):
                act.wait_ge(y_ready, t + 1)
                dst = o["y_prompt"][0, t0:t0 + c] if t < 2 else o["y_sample"][0]
                act.dma_start(dst, yacc[0:c, t, :]).then_inc(y_stored, 16)
            act.wait_ge(y_stored, 48)

        @block.gpsimd
        def _(pool):
            cc = Chain(pool, h["hc_pool"], 12)
            pc = Chain(pool, h["hp_pool"], 6)

            def key_decay(i, b):
                n = 2 * i + b
                cc.turn(n)
                pool.wait_ge(h["b_ready"], n + 1)
                for lv, hs in enumerate(LV):
                    w = SEQ if lv == 0 else T
                    xv = X[b][:, XO[lv]:XO[lv] + w].rearrange("p (m s) -> p m s", s=2 * hs)[:, :, 0:hs]
                    bv = hb[:, 0:w].rearrange("p (m s) -> p m s", s=2 * hs)
                    ins = pool.tensor_tensor(xv, bv[:, :, hs - 1:hs].to_broadcast([P, w // (2 * hs), hs]), bv[:, :, 0:hs], ALU.subtract)
                    if lv < 6:
                        cc(ins)
                signal(pool, ins, h["dl_ready"], n + 1)

            def key_side(i, b):
                n = 2 * i + b
                pool.wait_ge(h["E_ready"], n + 1)
                pool.wait_ge(h["k_ready"], n + 1)
                for lv, hs in enumerate(LV):
                    w = SEQ if lv == 0 else T
                    xv = X[b][:, XO[lv]:XO[lv] + w].rearrange("p (m s) -> p m s", s=2 * hs)[:, :, 0:hs]
                    kv = hk[:, b, 0:w].rearrange("p (m s) -> p m s", s=2 * hs)[:, :, 0:hs]
                    ins = pool.tensor_tensor(xv, xv, kv, ALU.mult)
                    if lv < 6:
                        cc(ins)
                signal(pool, ins, h["xl_ready"], n + 1)
                cc.end()

            def level_sums(i, b, tiles, first):
                n = 2 * i + b
                if tiles[0] == 0:
                    pc.turn(n)
                for t in tiles:
                    w = TILES[t][1]
                    pool.wait_ge(h["am_ready"], 3 * n + t + 1)
                    am = hAM[(b + t) % 2][0:w]
                    if t == 0 and not first:
                        pool.wait_ge(h["o_done"], n)
                    lo = 0 if t < 2 else 1
                    left = 4 if t < 2 else 3
                    pc(pool.tensor_tensor(am[:, lo:lo + left, 0:w], am[:, lo:lo + left, 0:w], am[:, lo + 4:lo + 4 + left, 0:w], ALU.add))
                    rest = 2
                    pc(pool.tensor_tensor(am[:, lo:lo + rest, 0:w], am[:, lo:lo + rest, 0:w], am[:, lo + 2:lo + 2 + rest, 0:w], ALU.add))
                    signal(pool, pool.tensor_tensor(hAS[0:w, t, 0:w], am[:, lo, 0:w], am[:, lo + 1, 0:w], ALU.add), h["as_ready"], 3 * n + t + 1)
                if tiles[-1] == 2:
                    pc.end()

            def head_turn(cur, prev, first_prev=False):
                if prev:
                    level_sums(*prev, [0], first_prev)
                if cur:
                    key_decay(*cur)
                if prev:
                    level_sums(*prev, [1], first_prev)
                if cur:
                    key_side(*cur)
                if prev:
                    level_sums(*prev, [2], first_prev)

            head_turn((0, 0), None)
            head_turn((0, 1), (0, 0), True)
            with pool.Fori(1, 4) as i:
                head_turn((i, 0), (i - 1, 1))
                head_turn((i, 1), (i, 0))
            head_turn(None, (3, 1))

        @block.vector
        def _(dve):
            step = Chain(dve, dve_step)
            step(dve.memset(one1[:, :], 1.0))
            step(dve.memset(eps1[:, :], EPS))
            step(dve.memset(mv[:, :, :], 1.0))
            step(dve.memset(ones, 1.0))
            signal(dve, dve.memset(uc[:, :, 0:HALO], 0.0), setup_done, 1)

            def norm_stats(halves, t, n, ch):
                for hf in range(2):
                    ch(dve.bn_stats(stats[0:n, t, hf, :], halves[hf]))

            def norm_apply(dst, src, t, n, g, b, rstd, ready, ch):
                ch(dve.scalar_tensor_tensor(dst, src, mv[0:n, t, 0:1], g, ALU.subtract, ALU.mult))
                dve.wait_ge(rstd, t + 1)
                signal(dve, dve.scalar_tensor_tensor(dst, dst, rstd3[0:n, t:t + 1], b, ALU.mult, ALU.add), ready, t + 1)

            for t, (_, n) in enumerate(TILES):
                dve.wait_ge(x_in[t], 16)
                norm_stats([x0[0:n, t, 0:512], x0[0:n, t, 512:1024]], t, n, step)
                ins = dve.bn_aggr(mv[0:n, t, :], stats[0:n, t, :, :].rearrange("p s n -> p (s n)"))
                signal(dve, ins, var0, t + 1)
            dve.wait_ge(gb0_in, 32)
            for t, (_, n) in enumerate(TILES):
                norm_apply(x0[0:n, t, :], x0[0:n, t, :], t, n, gb0[0:n, 0, :], gb0[0:n, 1, :], rstd0, x0_ready, step)

            dve.wait_ge(mask_in, 16)
            step(dve.tensor_copy(mask[:, :, :].rearrange("p l n -> p (l n)"), maskf))
            dve.wait_ge(rowsT_done, 1)
            step(dve.tensor_copy(vt[:, :, :].rearrange("p c n -> p (c n)"), ps[:, 7, 0:256]))
            step(dve.tensor_copy(hv[:, :], ps[:, 7, 256:265]))
            step(dve.tensor_tensor(lb[:, :], hv[:, 0:8], hv[:, 0:8], ALU.subtract))
            signal(dve, dve.tensor_scalar(olb[:, :], lb[:, :], -1.0, 1.0, ALU.mult, ALU.add), params_ready, 1)

            dve.wait_ge(x0T_done, 6)
            cc = Chain(dve, h["hc_dve"], 15)
            pc = Chain(dve, h["hp_dve"], 1)

            def forget_in(i, b, first):
                n = 2 * i + b
                cc.turn(n)
                dve.wait_ge(h["w_ready"], n + 1)
                cc(dve.scalar_tensor_tensor(hls, ps[:, 0, 0:T], 0.0, he, ALU.min, ALU.subtract))
                if not first:
                    dve.wait_ge(h["a_done"], 3 * n - 3)
                signal(dve, dve.tensor_tensor(hk[:, b, :], hls, ps[:, 0, 0:T], ALU.subtract), h["ls_ready"], n + 1)
                cc(dve.tensor_tensor(hls, hls, hw, ALU.add))
                if not (first and b == 0):
                    dve.wait_ge(h["kde_ready"], 3 * n)
                    dve.wait_ge(h["dl_ready"], n)
                signal(dve, dve.tensor_tensor_scan(hb, reset, hls, 0.0, ALU.mult, ALU.add), h["b_ready"], n + 1)

            def level_decay(i, b):
                n = 2 * i + b
                for lv, hs in enumerate(LV):
                    w = SEQ if lv == 0 else T
                    xv = X[b][:, XO[lv]:XO[lv] + w].rearrange("p (m s) -> p m s", s=2 * hs)
                    bv = hb[:, 0:w].rearrange("p (m s) -> p m s", s=2 * hs)
                    ins = dve.tensor_tensor(xv[:, :, hs:2 * hs], bv[:, :, hs:2 * hs], bv[:, :, hs - 1:hs].to_broadcast([P, w // (2 * hs), hs]), ALU.subtract)
                    if lv < 6:
                        cc(ins)
                signal(dve, ins, h["dr_ready"], n + 1)

            def key_scale(i, b):
                n = 2 * i + b
                dve.wait_ge(h["kexp_ready"], n + 1)
                signal(dve, dve.tensor_scalar(hk[:, b, :], hk[:, b, :], olb[:, bass.ds(n, 1)], None, ALU.mult), h["k_ready"], n + 1)

            def g_clamp(i, b):
                n = 2 * i + b
                dve.wait_ge(h["g_done"], n + 1)
                signal(dve, dve.tensor_scalar(hgx, ps[:, 2, 0:T], -40.0, None, ALU.max), h["gc_ready"], n + 1)

            def g_silu(i, b):
                n = 2 * i + b
                dve.wait_ge(h["gx_ready"], n + 1)
                signal(dve, dve.tensor_tensor(hsg[:, b, :], ps[:, 2, 0:T], hgx, ALU.mult), h["sg_ready"], n + 1)

            def query_side(i, b):
                n = 2 * i + b
                dve.wait_ge(h["E_ready"], n + 1)
                dve.wait_ge(h["q_sb"], n + 1)
                for lv, hs in enumerate(LV):
                    w = SEQ if lv == 0 else T
                    xv = X[b][:, XO[lv]:XO[lv] + w].rearrange("p (m s) -> p m s", s=2 * hs)[:, :, hs:2 * hs]
                    qv = hq[:, b, 0:w].rearrange("p (m s) -> p m s", s=2 * hs)[:, :, hs:2 * hs]
                    ins = dve.tensor_tensor(xv, xv, qv, ALU.mult)
                    if lv < 6:
                        cc(ins)
                signal(dve, ins, h["xr_ready"], n + 1)

            def carry_side(i, b, first):
                n = 2 * i + b
                dve.wait_ge(h["kde_ready"], 3 * n + 3)
                cc(dve.tensor_copy(hebl[:, b, :], heb[:, SEQ - 1:T:DEC]))
                if not first:
                    dve.wait_ge(h["o_done"], n)
                signal(dve, dve.tensor_tensor(hqeb, heb, hq[:, b, :], ALU.mult), h["qeb_ready"], n + 1)
                signal(dve, dve.tensor_tensor(hkde, hkde, hk[:, b, :], ALU.mult), h["kdec_ready"], n + 1)
                cc.end()

            def level_mask(i, b, t, first):
                n = 2 * i + b
                w = TILES[t][1]
                dve.wait_ge(h["a_done"], 3 * n + t + 1)
                if not (first and t < 2):
                    dve.wait_ge(h["as_ready"], 3 * n + t - 1)
                pv = ps[:, 4:6, :].rearrange("p b (l n) -> p (b l) n", l=4)
                lo = 0 if t < 2 else 1
                signal(dve, dve.tensor_tensor(hAM[(b + t) % 2][0:w, lo:8, 0:w], pv[0:w, lo:8, 0:w], mask[0:w, lo:8, 0:w], ALU.mult), h["am_ready"], 3 * n + t + 1)

            def prev_final(i, b, first):
                n = 2 * i + b
                pc.turn(n)
                dve.wait_ge(h["sa_sb"], n + 1)
                if not first:
                    dve.wait_ge(h["so_stored"], 32 * n)
                pc(dve.scalar_tensor_tensor(hSo[:, 0, :], hSA, hebl[:, b, 0:1], ps[:, 7, P:2 * P], ALU.mult, ALU.add))
                dve.wait_ge(st_in[b], i * 16 + 16)
                signal(dve, dve.scalar_tensor_tensor(hSo[:, 1, :], hSst[:, b, :], hebl[:, b, 1:2], ps[:, 7, 2 * P:3 * P], ALU.mult, ALU.add), h["so_ready"], n + 1)
                pc.end()

            oc = Chain(dve, h["ho_dve"], 1)

            def pprev_out(i, b):
                n = 2 * i + b
                oc.turn(n)
                dve.wait_ge(h["rstd_exp"], n + 1)
                oc(dve.scalar_tensor_tensor(hrs, ps[:, 6, 0:T], hv[:, 8:9], hrs, ALU.mult, ALU.mult))
                signal(dve, dve.tensor_tensor(oT[:, bass.ds(n, 1), :].rearrange("p o n -> p (o n)"), hrs, hsg[:, b, :], ALU.mult), h["o_out"], n + 1)

            def head_turn(cur, prev, pprev, first=False, first_prev=False):
                if cur:
                    forget_in(*cur, first or first_prev)
                if prev:
                    level_mask(*prev, 0, first_prev)
                if cur:
                    level_decay(*cur)
                if pprev:
                    pprev_out(*pprev)
                if prev:
                    level_mask(*prev, 1, first_prev)
                if cur:
                    key_scale(*cur)
                    g_clamp(*cur)
                if prev:
                    level_mask(*prev, 2, first_prev)
                if cur:
                    query_side(*cur)
                    g_silu(*cur)
                if prev:
                    prev_final(*prev, first_prev)
                if cur:
                    carry_side(*cur, first)

            head_turn((0, 0), None, None, first=True)
            head_turn((0, 1), (0, 0), None, first_prev=True)
            with dve.Fori(1, 4) as i:
                head_turn((i, 0), (i - 1, 1), (i - 1, 0))
                head_turn((i, 1), (i, 0), (i - 1, 1))
            level_mask(3, 1, 0, False)
            pprev_out(3, 0)
            level_mask(3, 1, 1, False)
            level_mask(3, 1, 2, False)
            prev_final(3, 1, False)

            vc = Chain(dve, conv_step)

            def conv_gate(c):
                b = c % 2
                vc(dve.tensor_copy(uc[:, c, HALO + SEQ:2 * HALO + SEQ], vt[:, c, 34:64]))
                dve.wait_ge(sgu_ready, c + 1)
                vc(dve.tensor_tensor(uc[:, c, HALO:HALO + SEQ], ps[:, U_BANKS[c][0], 0:SEQ], sgu[:, b, 0:SEQ], ALU.mult))
                signal(dve, dve.tensor_tensor(uc[:, c, 2 * HALO + SEQ:UW], ps[:, U_BANKS[c][0], SEQ:T], sgu[:, b, SEQ:T], ALU.mult), u_ready, c + 1)

            HALF = TAPS // 2

            def conv_taps_a(c):
                vc(dve.tensor_copy(utail[:, c, 0, :], uc[:, c, SEQ:SEQ + HALO]))
                vc(dve.tensor_copy(utail[:, c, 1, :], uc[:, c, UW - HALO:UW]))
                vc(dve.tensor_scalar(acc, uc[:, c, 0:CW], vt[:, c, 0:1], vt[:, c, 31:32], ALU.mult, ALU.add))
                for j in range(1, HALF):
                    vc(dve.scalar_tensor_tensor(acc, uc[:, c, j:j + CW], vt[:, c, j:j + 1], acc, ALU.mult, ALU.add))

            def conv_taps_b(c):
                for j in range(HALF, TAPS - 1):
                    vc(dve.scalar_tensor_tensor(acc, uc[:, c, j:j + CW], vt[:, c, j:j + 1], acc, ALU.mult, ALU.add))
                signal(dve, dve.scalar_tensor_tensor(cT[:, c, :], uc[:, c, TAPS - 1:TAPS - 1 + CW], vt[:, c, TAPS - 1:TAPS], acc, ALU.mult, ALU.add),
                       conv_done, c + 1)

            def tail(i, b):
                n = 2 * i + b
                dve.wait_ge(sgt_ready, 2 * n + 2)
                signal(dve, dve.tensor_tensor(mT[:, bass.ds(n, 1), :].rearrange("p o n -> p (o n)"), ps[:, 3 * b + 2, 0:T], sgt[:, b, :], ALU.mult), m_ready, n + 1)

            conv_gate(0)
            pprev_out(3, 1)
            conv_taps_a(0)
            conv_taps_b(0)
            conv_gate(1)
            conv_gate(2)
            conv_gate(3)
            conv_taps_a(1)
            conv_taps_b(1)
            tail(0, 0)
            conv_taps_a(2)
            tail(0, 1)
            conv_taps_b(2)
            tail(1, 0)
            conv_taps_a(3)
            tail(1, 1)
            conv_taps_b(3)
            tail(2, 0)
            tail(2, 1)

            dve.wait_ge(cmean_done, 1)
            step(dve.tensor_scalar(crs, ps[:, 6, 0:CW], 1.0 / DB, None, ALU.mult))
            for c in range(CT):
                ins = dve.tensor_tensor(cT[:, c, :], cT[:, c, :], crs, ALU.subtract)
                if c < CT - 1:
                    step(ins)
            signal(dve, ins, cdiff_ready, 1)
            tail(3, 0)
            dve.wait_ge(crs_ready, 1)
            for c in range(CT):
                ins = dve.tensor_tensor(cT[:, c, :], cT[:, c, :], crs, ALU.mult)
                if c < CT - 1:
                    step(ins)
            signal(dve, ins, cz_ready, 1)
            tail(3, 1)
            step(dve.tensor_scalar(alI, ident, ALPHA, None, ALU.mult))

            bc = Chain(dve, mb_step)
            for d in range(KT):
                dve.wait_ge(yb_done, d + 1)
                bc(dve.tensor_tensor(t12[:, d % 2, :], ps[:, (1, 2, 4, 5)[d % 4], 0:T], sgb[:, d, :], ALU.mult))
                signal(dve, dve.tensor_tensor(mT[:, d, :], mT[:, d, :], t12[:, d % 2, :], ALU.add), mb_ready, d + 1)

            def stats1(t, n):
                dve.wait_ge(mix_done, t + 1)
                norm_stats([ps[0:n, 2 * t, :], ps[0:n, 2 * t + 1, :]], t, n, step)
                signal(dve, dve.bn_aggr(mv[0:n, t, :], stats[0:n, t, :, :].rearrange("p s n -> p (s n)")), var1, t + 1)

            def apply1(t, n):
                norm_apply(x1[0:n, t, :], ps[0:n, 2 * t:2 * t + 2, :].rearrange("p b n -> p (b n)"), t, n, gb1[0:n, 0, :], gb1[0:n, 1, :], rstd1, x1_ready, step)

            dve.wait_ge(gb1_in, 32)
            stats1(0, 128)
            apply1(0, 128)
            stats1(1, 128)
            apply1(1, 128)
            stats1(2, 64)
            apply1(2, 64)

            rs = Chain(dve, route_step)
            rs(dve.memset(L16, 0.0))
            dve.wait_ge(logit_done, 1)
            for t, (_, n) in enumerate(TILES):
                rs(dve.tensor_copy(L16[0:n, t, :], ps[0:n, 4, t * NE:t * NE + NE]))
            mx = cnt[:, 0:3]
            w3 = [P, 3, NE]

            def b3(v):
                return v.rearrange("p (t o) -> p t o", o=1).to_broadcast(w3)

            def bi(v):
                return v.rearrange("p (o n) -> p o n", o=1).to_broadcast(w3)

            rs(dve.tensor_reduce(mx, L16, AX_X, ALU.max))
            signal(dve, dve.tensor_tensor(L16, L16, b3(mx), ALU.subtract), lmax_ready, 1)
            dve.wait_ge(lexp_ready, 1)
            rs(dve.tensor_reduce(mx, L16, AX_X, ALU.add))
            rs(dve.reciprocal(mx, mx))
            rs(dve.tensor_tensor(S16, L16, b3(mx), ALU.mult))
            dve.wait_ge(rb_in, 16)
            rs(dve.tensor_tensor(Z16, S16, bi(rb), ALU.add))
            zg = Z16.rearrange("p t (g s) -> p (t g) s", g=GR)
            rs(dve.tensor_tensor(PS6[:, :, 0:3], zg[:, :, 0:3], zg[:, :, 1:4], ALU.add))
            rs(dve.tensor_tensor(PS6[:, :, 3:5], zg[:, :, 0:2], zg[:, :, 2:4], ALU.add))
            rs(dve.tensor_tensor(PS6[:, :, 5:6], zg[:, :, 0:1], zg[:, :, 3:4], ALU.add))
            gsc, gone = G3[:, 0:3, :], G3[:, 3:6, :]
            rs(dve.tensor_reduce(gsc.rearrange("p t g -> p (t g)"), PS6, AX_X, ALU.max))

            def first_best(score, one, idx, n, work):
                wide = [P, 3, n]
                bb = lambda v: v.rearrange("p (t o) -> p t o", o=1).to_broadcast(wide)
                ib = idx.rearrange("p (o n) -> p o n", o=1).to_broadcast(wide)
                rs(dve.tensor_reduce(mx, score, AX_X, ALU.max))
                rs(dve.tensor_tensor(one, score, bb(mx), ALU.is_equal))
                rs(dve.tensor_scalar(work, one, -1.0e3, 1.0e3, ALU.mult, ALU.add))
                rs(dve.tensor_tensor(work, work, ib, ALU.add))
                rs(dve.tensor_reduce(mx, work, AX_X, ALU.min))
                rs(dve.tensor_tensor(one, work, bb(mx), ALU.is_equal))

            first_best(gsc, gone, i4, GR, G4[:, 0:3, :])
            def by_group(v):
                return v.rearrange("p t (g o) -> p (t g) o", o=1).to_broadcast([P, 3 * GR, NE // GR])

            mg = M16.rearrange("p t (g s) -> p (t g) s", g=GR)
            rs(dve.tensor_tensor(mg, zg, by_group(gone), ALU.mult))
            rs(dve.tensor_scalar(G4[:, 0:3, :], gone, -MASK_SCORE, MASK_SCORE, ALU.mult, ALU.add))
            rs(dve.tensor_tensor(mg, mg, by_group(G4[:, 0:3, :]), ALU.add))
            first_best(M16, O1, i16, NE, N16)
            rs(dve.scalar_tensor_tensor(M16, O1, -1.0e9, M16, ALU.mult, ALU.add))
            first_best(M16, O2, i16, NE, N16)
            rs(dve.tensor_tensor(O1, O1, O2, ALU.add))
            rs(dve.tensor_tensor(GT16, O1, S16, ALU.mult))
            rs(dve.tensor_reduce(mx, GT16, AX_X, ALU.add))
            rs(dve.reciprocal(mx, mx))
            rs(dve.tensor_tensor(rt[:, 2], GT16, b3(mx), ALU.mult))
            rs(dve.memset(O1[64:128, 2, :], 0.0))
            rs(dve.memset(rt[64:128, 2, 2, :], 0.0))
            signal(dve, dve.tensor_copy(rt[:, 1], O1), chosen, 1)
            dve.wait_ge(pos_done, 1)
            rs(dve.tensor_copy(rt[:, 0], ps[:, 5, 0:3 * NE].rearrange("p (t n) -> p t n", t=3)))
            rs(dve.tensor_reduce(cnt[:, 4:5], ps[:, 5, 3 * NE:4 * NE], AX_X, ALU.max))
            rs(dve.tensor_scalar(cnt[:, 5:6], cnt[:, 4:5], float(CAP), None, ALU.is_gt))
            signal(dve, dve.tensor_copy(flag, cnt[:, 5:6]), routed, 1)

            ec = Chain(dve, e["e_dve"], 11)

            def picks(n, p):
                ec.turn(n)
                ec(dve.tensor_copy(cur, rt[:, :, :, bass.ds(2 * p, 2)]))
                for t in range(3):
                    for m in range(2):
                        pick = ec if (t, m) != (2, 1) else lambda ins: signal(dve, ins, e["pick_ready"], n + 1)
                        pick(dve.tensor_scalar(ePm[:, t, 64 * m:64 * m + 64], i64, cur[:, 0, t, m:m + 1], cur[:, 1, t, m:m + 1], ALU.is_equal, ALU.mult))
                for t in range(3):
                    for m in range(2):
                        ins = dve.tensor_scalar(eGm[:, t, 64 * m:64 * m + 64], i64, cur[:, 0, t, m:m + 1], cur[:, 2, t, m:m + 1], ALU.is_equal, ALU.mult)
                        if (t, m) != (2, 1):
                            ec(ins)
                signal(dve, ins, e["gpick_ready"], n + 1)
                ec.end()

            def expert_pair(n, p):
                picks(n, p)
                dve.wait_ge(e["eXT_done"], n + 1)
                signal(dve, dve.tensor_copy(eXT[:, 4:8, :], ps[:, 5, :].rearrange("p (k n) -> p k n", k=4)), e["eXT_b"], n + 1)
                dve.wait_ge(e["group_used"], 6 * n + 4)
                dve.wait_ge(e["silu_ready"], n + 1)
                signal(dve, dve.tensor_tensor(eh, ehs, ps[:, 2:4, :].rearrange("p b n -> p (b n)"), ALU.mult), e["eh_ready"], n + 1)
                dve.wait_ge(e["ehT_done"], n + 1)
                signal(dve, dve.tensor_copy(ehT[:, 4:8, :], ps[:, 5, :].rearrange("p (k n) -> p k n", k=4)), e["ehT_b"], n + 1)
                for t, (_, c) in enumerate(TILES):
                    for hf in range(2):
                        j = 2 * t + hf
                        dve.wait_ge(e["y_done"], 6 * n + j + 1)
                        yv = yacc[0:c, t, hf * 512:hf * 512 + 512]
                        signal(dve, dve.tensor_tensor(yv, yv, ps[0:c, 2 + j % 4, :], ALU.add), e["y_added"], 6 * n + j + 1)

            dve.wait_ge(yacc_ready, 3)
            dve.wait_ge(tail_stored, 32)
            with dve.Fori(0, PAIRS) as p:
                expert_pair(p, p)
            more = dve.value_load(flag[0:1, :], min_val=0, max_val=1)
            with dve.If(more != 0):
                with dve.Fori(1, ROUNDS) as r:
                    dve.tensor_scalar(rt[:, 0], rt[:, 0], float(-CAP), None, ALU.add).then_inc(h["round"], 1)
                    with dve.Fori(0, PAIRS) as p:
                        dve.wait_ge(h["round"], r)
                        expert_pair(PAIRS * r + p, p)

            ns = Chain(dve, norm_step)

            def stats2(t, n):
                norm_stats([yacc[0:n, t, 0:512], yacc[0:n, t, 512:1024]], t, n, ns)
                signal(dve, dve.bn_aggr(mv[0:n, t, :], stats[0:n, t, :, :].rearrange("p s n -> p (s n)")), var2, t + 1)

            def apply2(t, n):
                norm_apply(yacc[0:n, t, :], yacc[0:n, t, :], t, n, g2[0:n, :], b2[0:n, :], rstd2, y_ready, ns)

            dve.wait_ge(gb2_in, 32)
            stats2(0, 128)
            apply2(0, 128)
            stats2(1, 128)
            apply2(1, 128)
            stats2(2, 64)
            apply2(2, 64)


_INS = ["x_prompt", "x_sample", "state_hgrn", "state_conv", "ln_in_g", "ln_in_b", "w_in", "lb_logits", "hg_norm_g", "w_o_a",
        "conv_w", "conv_b", "cn_g", "cn_b", "w_o_b", "w_out", "ln1_g", "ln1_b", "w_router", "router_bias", "w_gate_e",
        "w_up_e", "w_down_e", "ln2_g", "ln2_b"]
_OUTS = [("y_prompt", (1, SEQ, D)), ("y_sample", (1, DEC, D)), ("new_hgrn_prompt", (1, 1, HEADS, P, P)), ("new_conv_prompt", (1, 1, HALO, DB)),
         ("new_hgrn_sample", (1, 1, HEADS, P, P)), ("new_conv_sample", (1, 1, HALO, DB))]


def kernel(**inputs):
    import numpy as _np
    import concourse.bacc as _bacc
    from concourse.bass_utils import run_bass_kernel_spmd as _run

    nc = _bacc.Bacc("TRN2", target_bir_lowering=False, num_devices=1)
    arrays, a, o = {}, {}, {}
    given = {n: _np.ascontiguousarray(inputs[n]) for n in _INS}
    given["consts"], given["masks"] = shape_constants()
    for name, v in given.items():
        arrays[f"in_{name}"] = v
        a[name] = nc.dram_tensor(f"in_{name}", v.shape, mybir.dt.from_np(v.dtype), kind="ExternalInput").ap()
    for name, shape in _OUTS:
        o[name] = nc.dram_tensor(f"out_{name}", shape, F32, kind="ExternalOutput").ap()
    build(nc, a, o)
    r = _run(nc, [arrays], core_ids=[0])
    return tuple(r.results[0][f"out_{name}"] for name, _ in _OUTS)
```

```python
from contextlib import ExitStack

import concourse.bass as bass
from concourse import mybir

F32 = mybir.dt.float32
F32R = mybir.dt.float32r
BF16 = mybir.dt.bfloat16
I32 = mybir.dt.int32
ALU = mybir.AluOpType
ACT = mybir.ActivationFunctionType
AX_X = mybir.AxisListType.X

P = 128
D = 1024
KT = D // P
SEQ, DEC = 256, 64
T = SEQ + DEC
HEADS = 8
DB = 512
CT = DB // P
TAPS = 31
HALO = TAPS - 1
UW = HALO + SEQ + HALO + DEC
CW = UW - HALO
NE = 16
GR = 4
CAP = 64
PAIRS = NE // 2
ROUNDS = T // CAP
RING = 4
EPS = 1e-5
ALPHA = 2.0 ** 0.25
QSCALE = float(P) ** -0.5
MASK_SCORE = -1.0e4
TILES = [(0, 128), (128, 128), (256, 64)]
LV = [64, 32, 16, 8, 4, 2, 1]
XO = [0] + [256 + i * T for i in range(6)]
XW = 256 + 6 * T
COFF = {"ident": 0, "reset": 128, "tri": 128 + T, "i64": 256 + T, "i16": 320 + T, "i4": 336 + T}
CWID = 340 + T
Q0, F0, V0, G0, UA0, UB0, GA0, GB0 = 0, D, 2 * D, 3 * D, 4 * D, 4 * D + DB, 5 * D, 6 * D


def shape_constants():
    import numpy as np

    c = np.zeros((P, CWID), np.float32)
    c[:, 0:P] = np.eye(P)
    c[:, COFF["reset"]:COFF["reset"] + T] = 1.0
    for t0, _ in TILES:
        c[:, COFF["reset"] + t0] = 0.0
    c[:, COFF["tri"]:COFF["tri"] + P] = np.triu(np.ones((P, P)), 1)
    c[:, COFF["i64"]:COFF["i64"] + CAP] = np.arange(CAP)
    c[:, COFF["i16"]:COFF["i16"] + NE] = np.arange(NE)
    c[:, COFF["i4"]:COFF["i4"] + GR] = np.arange(GR)
    s, t = np.arange(P)[:, None], np.arange(P)[None, :]
    m = [(s // (2 * h) == t // (2 * h)) & (s % (2 * h) < h) & (t % (2 * h) >= h) for h in LV]
    m.append(s == t)
    return c, np.stack(m, 1).reshape(P, 8 * P).astype(np.float32)


X0_BANKS = [0, 1, 2, 3, 0, 1]
X1_BANKS = [6, 7, 0, 1, 2, 3]
U_BANKS = [(0, 1), (2, 3), (5, 7), (0, 1)]


class Chain:

    def __init__(self, eng, sem, per=0):
        self.eng, self.sem, self.per, self.base, self.n = eng, sem, per, 0, 0

    def turn(self, i):
        self.base, self.n = (i * self.per if self.per else 0), 0

    def __call__(self, ins):
        self.n += 1
        ins.then_inc(self.sem, 1)
        self.eng.wait_ge(self.sem, self.base + self.n)

    def end(self):
        assert self.n == self.per, (self.n, self.per)


def signal(eng, ins, sem, value):
    ins.then_inc(sem, 1)
    eng.wait_ge(sem, value)


def build(nc, a, o):
    with ExitStack() as ctx:
        def sb(name, shape, dt=F32):
            return ctx.enter_context(nc.sbuf_tensor(name, shape, dt))

        def sem(name):
            return ctx.enter_context(nc.semaphore(name))

        with ExitStack() as early:
            x_at, w_at = 8 * D, 16 * D
            split_t, split_x, _, split_w = (early.enter_context(nc.sbuf_tensor(name, [P, n], F32R)) for name, n in (
                ("split_t", x_at), ("split_x", 2 * KT * T), ("split_gap", w_at - x_at - 2 * KT * T), ("split_w", 6 * D)))
        ring = sb("ring", [P, RING, 2, 4, D])
        slots = ring[:, RING - 1].rearrange("p b k n -> p b (k n)")
        cst = sb("cst", [P, CWID])
        ones_t = sb("ones", [P, P])
        ones = ones_t[:, :]
        xT = sb("xT", [P, KT, T])
        mid = sb("mid", [P, KT * T + CT * CW + 4 * P])
        oT = mid[:, 0:KT * T].rearrange("p (k n) -> p k n", k=KT)
        cT = mid[:, KT * T:KT * T + CT * CW].rearrange("p (c n) -> p c n", c=CT)
        mask = mid[:, KT * T + CT * CW:].bitcast(BF16).rearrange("p (l n) -> p l n", l=8)
        vt = sb("vt", [P, CT, 64])
        hv = sb("hv", [P, 9])
        lb = sb("lb", [P, 8])
        olb = sb("olb", [P, 8])
        utail = sb("utail", [P, CT, 2, HALO])
        stats = sb("stats", [P, 3, 2, 6])
        mv = sb("mv", [P, 3, 2])
        rstd3 = sb("rstd3", [P, 3])
        one1 = sb("one1", [P, 1])
        eps1 = sb("eps1", [P, 1])
        AR = 11950
        ar = sb("ar", [P, AR])
        ps = ctx.enter_context(nc.psum_tensor("ps", [P, 8, 512], F32))

        def carve(first, *sizes):
            out, at = [], first
            for n in sizes:
                out.append(ar[:, at:at + n])
                at += n
            assert at <= AR, at
            return out

        ident = cst[:, 0:P]
        reset = cst[:, COFF["reset"]:COFF["reset"] + T]
        tri = cst[:, COFF["tri"]:COFF["tri"] + P]
        i64 = cst[:, COFF["i64"]:COFF["i64"] + CAP]
        i16 = cst[:, COFF["i16"]:COFF["i16"] + NE]
        i4 = cst[:, COFF["i4"]:COFF["i4"] + GR]

        x0f, gb0, rows_a, hrows_a, maskf = carve(0, 3 * D, 2 * D, DB, P, 8 * P)
        x0 = x0f.rearrange("p (t n) -> p t n", t=3)
        gb0 = gb0.rearrange("p (g n) -> p g n", g=2)
        ucf, sgu_f, acc, alI = carve(9100, CT * UW, 2 * T, CW, P)
        uc = ucf.rearrange("p (b n) -> p b n", b=CT)
        sgu = sgu_f.rearrange("p (b n) -> p b n", b=2)
        (hq, hk, hsg, hV, he, hw, hls, hb, hgx, heb, hqeb, hkde, hkT, hAM0, hAM1, hAS, hSA, hSst, hSo, hosq, hrs, hebl) = carve(
            0, 2 * T, 2 * T, 2 * T, 384, T, T, T, T, T, T, T, T, 384, 1024, 1024, 384, P, 2 * P, 2 * P, T, T, 4)
        two = lambda v: v.rearrange("p (b n) -> p b n", b=2)
        hq, hk, hsg, hSst, hSo, hebl = two(hq), two(hk), two(hsg), two(hSst), two(hSo), two(hebl)
        hV, hkT, hAS = (v.rearrange("p (b n) -> p b n", b=3) for v in (hV, hkT, hAS))
        hAM = [v.rearrange("p (l n) -> p l n", l=8) for v in (hAM0, hAM1)]
        X = [ring[:, 0, b].rearrange("p k n -> p (k n)")[:, 0:XW] for b in range(2)]
        mTf, sgbf, sgtf, t12f, cnf, csq = carve(0, KT * T, KT * T, 2 * T, 2 * T, CT * T, CT * CW)
        gb1f, ncv = carve(7680, 2 * D, 2 * DB)
        crs = acc
        mT = mTf.rearrange("p (k n) -> p k n", k=KT)
        sgb = sgbf.rearrange("p (k n) -> p k n", k=KT)
        sgt = sgtf.rearrange("p (b n) -> p b n", b=2)
        t12 = t12f.rearrange("p (b n) -> p b n", b=2)
        cn = cnf.rearrange("p (c n) -> p c n", c=CT)
        csq = csq.rearrange("p (c n) -> p c n", c=CT)
        ncv = ncv.rearrange("p (s n) -> p s n", s=2)
        gb1 = gb1f.rearrange("p (g n) -> p g n", g=2)
        x1 = mid[:, 0:3 * D].rearrange("p (t n) -> p t n", t=3)
        g2 = mid[:, 3 * D:4 * D]
        x1T = xT
        b2, yaccf, wrt, rb, L16, S16, Z16, M16, N16, O1, O2, GT16, PS6, G3, G4, rt, cur, cnt, cnti, eXT, ehs, eh, ehT, eos, ePm, eGm, eGT = carve(
            0, D, 3 * D, KT * NE, NE, *[48] * 8, 72, 24, 24, 144, 18, 20, 4, KT * P, D, D, KT * P, D, 384, 384, 384)
        yacc = yaccf.rearrange("p (t n) -> p t n", t=3)
        eXT, ehT = (v.rearrange("p (k n) -> p k n", k=KT) for v in (eXT, ehT))
        ePm, eGm, eGT = (v.rearrange("p (t n) -> p t n", t=3) for v in (ePm, eGm, eGT))
        wrt = wrt.rearrange("p (k n) -> p k n", k=KT)
        L16, S16, Z16, M16, N16, O1, O2, GT16 = (v.rearrange("p (t n) -> p t n", t=3) for v in (L16, S16, Z16, M16, N16, O1, O2, GT16))
        PS6 = PS6.rearrange("p (m s) -> p m s", s=6)
        G3 = G3.rearrange("p (t g) -> p t g", t=6)
        G4 = G4.rearrange("p (t g) -> p t g", t=6)
        rt = rt.rearrange("p (w t n) -> p w t n", w=3, t=3)
        cur = cur.rearrange("p (w t e) -> p w t e", w=3, t=3)
        flag = cnti[:, 0:1].bitcast(I32)

        const_in, mask_in, rows_in, hrows_in, gb0_in = (sem(n) for n in ("const_in", "mask_in", "rows_in", "hrows_in", "gb0_in"))
        x_in = [sem(f"x_in{t}") for t in range(3)]
        setup_done, dve_step, act_step = sem("setup_done"), sem("dve_step"), sem("act_step")
        var0, rstd0, x0_ready, x0T_done, x0T_sb = (sem(n) for n in ("var0", "rstd0", "x0_ready", "x0T_done", "x0T_sb"))
        rowsT_done, params_ready = sem("rowsT_done"), sem("params_ready")
        wu_in = [sem(f"wu_in{c}") for c in range(CT)]
        u_done, sgu_ready, u_ready, conv_done, conv_step = (sem(n) for n in ("u_done", "sgu_ready", "u_ready", "conv_done", "conv_step"))
        xh_ready, xl_ready, whi_ready, wlo_ready, uhi_ready, ulo_ready, thi_ready, tlo_ready = (
            sem(n) for n in ("xh_ready", "xl_ready", "whi_ready", "wlo_ready", "uhi_ready", "ulo_ready", "thi_ready", "tlo_ready"))
        wg_in = [sem(f"wg_in{b}") for b in range(2)]
        wb_in = sem("wb_in")
        yb_done, mb_ready, mb_step = sem("yb_done"), sem("mb_ready"), sem("mb_step")
        wh_in = [sem(f"wh_in{b}") for b in range(2)]
        st_in = [sem(f"st_in{b}") for b in range(2)]
        names = ("f_done q_done g_done v_done e_ready ls_ready w_ready k_ready b_ready dr_ready dl_ready kexp_ready E_ready q_sb gc_ready gx_ready sg_ready "
                 "eb_ready kde_ready xr_ready xk_ready a_done am_ready as_ready qeb_ready kdec_ready kT_done kT_sb s_done sa_sb o_done "
                 "osq_ready rms_done rstd_ready rstd_exp o_out so_ready so_stored hc_dve hp_dve hc_act hp_act hc_pool hp_pool ho_dve v_sb round")
        h = {n: sem(n) for n in names.split()}
        tailT_done, tail_sb, tail_stored = sem("tailT_done"), sem("tail_sb"), sem("tail_stored")
        cmean_done, cdiff_ready, csq_ready, cvar_done, crs_ready, cz_ready, cn_ready = (
            sem(n) for n in ("cmean_done", "cdiff_ready", "csq_ready", "cvar_done", "crs_ready", "cz_ready", "cn_ready"))
        wt_in = [sem(f"wt_in{b}") for b in range(2)]
        t_done, sgt_ready, m_ready = sem("t_done"), sem("sgt_ready"), sem("m_ready")
        wo_in = sem("wo_in")
        gb1_in, gb2_in, wrt_in, rb_in = (sem(n) for n in ("gb1_in", "gb2_in", "wrt_in", "rb_in"))
        mix_done, var1, rstd1, x1_ready, x1T_done, x1T_sb = (sem(n) for n in ("mix_done", "var1", "rstd1", "x1_ready", "x1T_done", "x1T_sb"))
        yacc_ready = sem("yacc_ready")
        logit_done, route_step, lmax_ready, lexp_ready, chosen, pos_done, routed = (
            sem(n) for n in ("logit_done", "route_step", "lmax_ready", "lexp_ready", "chosen", "pos_done", "routed"))
        group_in = [sem(f"group_in{g}") for g in range(RING)]
        names = ("group_used pick_ready gpick_ready eXT_done eXT_a eXT_b eGT_done eGT_sb silu_ready eh_ready ehT_done ehT_a ehT_b "
                 "eos_ready y_done y_added e_dve")
        e = {n: sem(n) for n in names.split()}
        var2, rstd2, y_ready, y_stored, norm_step = (sem(n) for n in ("var2", "rstd2", "y_ready", "y_stored", "norm_step"))

        w_in, w_oa, w_ob, w_out = a["w_in"][0], a["w_o_a"][0], a["w_o_b"][0], a["w_out"][0]
        w_in_k = w_in.rearrange("(k p) n -> p k n", p=P)
        w_oa_k = w_oa.rearrange("(k p) n -> p k n", p=P)
        w_ob_k = w_ob.rearrange("(k p) n -> p k n", p=P)
        w_out_k = w_out.rearrange("(k p) n -> p k n", p=P)
        su = ring[:, 3].rearrange("p b k n -> p (b k n)").rearrange("p (c s k n) -> p c s k n", c=CT, s=2, k=KT)
        def parts(tensor, first, n):
            v = tensor[:, first:first + n]
            return v.bitcast(F32), v

        rf = ring[:, :, :, :, :].rearrange("p g b k n -> p (g b k n)")
        SLOT, PC = 8 * D, D
        xhF, xh = parts(split_x, 0, KT * T)
        _, xl = parts(split_x, KT * T, KT * T)
        whF, wh = parts(split_w, 0, 3 * PC)
        _, wl = parts(split_w, 3 * PC, 3 * PC)
        pieces = [[parts(split_t, (4 * bb + q) * PC, PC) for q in range(4)] for bb in range(2)]
        t_hi, t_lo = [z[0:2] for z in pieces], [z[2:4] for z in pieces]
        piece = lambda v, q: v[:, q * PC:q * PC + PC]
        u_hi = [[(piece(whF, q), piece(wh, q)) for q in range(2)], t_hi[0]]
        u_lo = [[(None, piece(wl, q)) for q in range(2)], t_lo[0]]
        xhk, xhkF, xlk = (v.rearrange("p (k n) -> p k n", k=KT) for v in (xh, xhF, xl))
        sh = slots[:, :, :].rearrange("p b (s k n) -> p b s k n", s=4, k=KT)
        stl = slots[:, :, 0:24 * P].rearrange("p b (k n) -> p b k n", n=P)
        so = ring[:, 2].rearrange("p b k n -> p (b k) n")
        sob = [rf[:, at:at + D] for at in (*[SLOT + 2 * KT * T + k * D for k in range(3)], 3 * SLOT + 3 * D)]
        xp = a["x_prompt"][0].rearrange("(t p) n -> t p n", p=P)
        xs = a["x_sample"][0]

        block = ctx.enter_context(nc.Block())

        def bcast(v, n):
            return v.rearrange("(o n) -> o n", o=1).to_broadcast([P, n])

        @block.sync
        def _(sp):
            sp.dma_start(x0[:, 0, :], xp[0]).then_inc(x_in[0], 16)
            sp.dma_start(x0[:, 1, :], xp[1]).then_inc(x_in[1], 16)
            sp.dma_start(x0[0:DEC, 2, :], xs).then_inc(x_in[2], 16)
            sp.dma_start(cst[:, :], a["consts"]).then_inc(const_in, 16)
            sp.dma_start(gb0[:, 0, :], bcast(a["ln_in_g"], D)).then_inc(gb0_in, 16)
            sp.dma_start(gb0[:, 1, :], bcast(a["ln_in_b"], D)).then_inc(gb0_in, 16)
            sp.dma_start(rows_a[0:TAPS, :], a["conv_w"][0]).then_inc(rows_in, 16)
            sp.dma_start(rows_a[31:32, :], a["conv_b"]).then_inc(rows_in, 16)
            sp.dma_start(rows_a[32:33, :], a["cn_g"]).then_inc(rows_in, 16)
            sp.dma_start(rows_a[33:34, :], a["cn_b"]).then_inc(rows_in, 16)
            sp.dma_start(rows_a[34:64, :], a["state_conv"][0, 0]).then_inc(rows_in, 16)
            sp.dma_start(hrows_a[0:8, :], a["lb_logits"].rearrange("o (h n) -> (o h) n", h=8)).then_inc(hrows_in, 16)
            sp.dma_start(hrows_a[8:9, :], a["hg_norm_g"]).then_inc(hrows_in, 16)
            def cols(first, c):
                return w_in_k[:, :, bass.ds(first + c * P, P)]

            def load_u(c):
                sp.dma_start(su[:, c, 0], cols(UA0, c)).then_inc(wu_in[c], 16)
                sp.dma_start(su[:, c, 1], cols(UB0, c)).then_inc(wu_in[c], 16)

            def load_head(i, b):
                c = 2 * i + b
                for s, first in enumerate((F0, Q0, G0, V0)):
                    sp.dma_start(sh[:, b, s], cols(first, c)).then_inc(wh_in[b], 16)

            def load_state(i, b):
                sp.dma_start(hSst[:, b, :], a["state_hgrn"][0, 0, bass.ds(2 * i + b, 1)].rearrange("o p n -> (o p) n")).then_inc(st_in[b], 16)

            def load_gates(i, b):
                c = 2 * i + b
                sp.dma_start(stl[:, b, 0:8], cols(GA0, c)).then_inc(wg_in[b], 16)
                sp.dma_start(stl[:, b, 8:16], cols(GB0, c)).then_inc(wg_in[b], 16)

            def load_oa(i, b):
                c = 2 * i + b
                sp.dma_start(stl[:, b, 16:24], w_oa_k[:, :, bass.ds(c * P, P)]).then_inc(wt_in[b], 16)

            load_head(0, 0)
            sp.dma_start(maskf, a["masks"]).then_inc(mask_in, 16)
            load_head(0, 1)
            sp.wait_ge(x0T_done, 6)
            for b in range(2):
                load_state(0, b)
            for k in range(3):
                sp.dma_start(sob[k], w_ob_k[:, k]).then_inc(wb_in, 16)
            with sp.Fori(1, 4) as i:
                for b in range(2):
                    sp.wait_ge(h["v_done"], 2 * i + b - 1)
                    load_head(i, b)
                    sp.wait_ge(h["so_ready"], 2 * i + b - 1)
                    sp.wait_ge(h["o_done"], 2 * i + b - 1)
                    load_state(i, b)
            for b in range(2):
                sp.wait_ge(h["v_done"], 7 + b)
                load_u(2 * b)
                load_u(2 * b + 1)
            for b in range(2):
                sp.wait_ge(ulo_ready, 4 * b + 4)
                load_gates(0, b)
                load_oa(0, b)
            sp.dma_start(sob[3], w_ob_k[:, 3]).then_inc(wb_in, 16)
            with sp.Fori(1, 4) as i:
                for b in range(2):
                    sp.wait_ge(tlo_ready, 4 * i + 2 * b - 2)
                    load_gates(i, b)
            sp.dma_start(so, w_out_k).then_inc(wo_in, 16)
            sp.wait_ge(cvar_done, 1)
            sp.dma_start(gb1[:, 0, :], bcast(a["ln1_g"][0], D)).then_inc(gb1_in, 16)
            sp.dma_start(gb1[:, 1, :], bcast(a["ln1_b"][0], D)).then_inc(gb1_in, 16)
            sp.wait_ge(cn_ready, 8)
            sp.dma_start(g2, bcast(a["ln2_g"][0], D)).then_inc(gb2_in, 16)

            wg, wu, wd = (a[n][0].rearrange("e (s k p) n -> s p e k n", p=P, s=2) for n in ("w_gate_e", "w_up_e", "w_down_e"))

            def load_group(i, g):
                src = (wg, wu, wd)[g % 6 // 2][g % 2]
                for m in range(2):
                    sp.dma_start(ring[:, g % RING, m], src[:, bass.ds(4 * i + 2 * (g // 6) + m, 1)].rearrange("p o k n -> p (o k) n")).then_inc(group_in[g % RING], 16)

            sp.wait_ge(t_done, 8)
            load_group(0, 0)
            sp.wait_ge(yb_done, 8)
            load_group(0, 1)
            load_group(0, 3)
            sp.wait_ge(mb_ready, 8)
            sp.dma_start(wrt, a["w_router"].rearrange("(k p) n -> p k n", p=P)).then_inc(wrt_in, 16)
            sp.dma_start(rb, bcast(a["router_bias"], NE)).then_inc(rb_in, 16)
            sp.wait_ge(mix_done, 3)
            load_group(0, 2)
            sp.dma_start(b2, bcast(a["ln2_b"][0], D)).then_inc(gb2_in, 16)
            for g in range(RING, 12):
                sp.wait_ge(e["group_used"], g - RING + 1)
                load_group(0, g)
            with sp.Fori(1, PAIRS // 2) as i:
                for g in range(12):
                    sp.wait_ge(e["group_used"], 12 * i + g - RING + 1)
                    load_group(i, g)
            sp.wait_ge(routed, 1)
            more = sp.value_load(flag[0:1, :], min_val=0, max_val=1)
            with sp.If(more != 0):
                with sp.Fori(1, ROUNDS) as r:
                    with sp.Fori(0, PAIRS // 2) as i:
                        for g in range(12):
                            sp.wait_ge(e["group_used"], 6 * PAIRS * r + 12 * i + g - RING + 1)
                            load_group(i, g)

        @block.tensor
        def _(pe):
            def mm(out, lhsT, rhs, start, stop):
                return pe.matmul(out, lhsT, rhs, start=start, stop=stop)

            pe.wait_ge(const_in, 16)
            pe.wait_ge(rows_in, 80)
            pe.wait_ge(hrows_in, 32)
            pe.wait_ge(setup_done, 1)
            for c in range(CT):
                pe.transpose(ps[:, 7, c * 64:c * 64 + 64], rows_a[0:64, c * P:c * P + P], ident[0:64, 0:64])
            pe.transpose(ps[:, 7, 256:265], hrows_a[0:9, :], ident[0:9, 0:9]).then_inc(rowsT_done, 1)

            def to_features(src, ready, done, copied, banks):
                for t, (_, n) in enumerate(TILES):
                    pe.wait_ge(ready, t + 1)
                    for hf in range(2):
                        bank = banks[2 * t + hf]
                        if bank in banks[:2 * t + hf]:
                            pe.wait_ge(copied, banks.index(bank) + 1)
                        for k in range(4):
                            last = pe.transpose(ps[:, bank, k * P:k * P + n], src[0:n, t, (4 * hf + k) * P:(4 * hf + k + 1) * P], ident[0:n, 0:n])
                        last.then_inc(done, 1)

            to_features(x0, x0_ready, x0T_done, x0T_sb, X0_BANKS)

            def project(bank, hi, lo):
                for k in range(KT):
                    for j, (w, x) in enumerate(((hi, xhk), (lo, xhk), (hi, xlk))):
                        last = mm(ps[:, bank, 0:T], w[:, k * P:k * P + P], x[:, k, :], k == 0 and j == 0, k == KT - 1 and j == 2)
                return last

            pe.wait_ge(x0T_sb, 6)
            pe.wait_ge(xl_ready, 6)

            def cur_f(i, b, first):
                pe.wait_ge(wlo_ready, 3 * (2 * i + b) + 1)
                if not first:
                    pe.wait_ge(h["ls_ready"], 2 * i + b)
                project(0, piece(wh, 0), piece(wl, 0)).then_inc(h["f_done"], 1)

            def cur_q(i, b, first):
                pe.wait_ge(wlo_ready, 3 * (2 * i + b) + 2)
                if not first:
                    pe.wait_ge(h["q_sb"], 2 * i + b)
                project(1, piece(wh, 1), piece(wl, 1)).then_inc(h["q_done"], 1)

            def cur_g(i, b, first, after_rms):
                pe.wait_ge(wlo_ready, 3 * (2 * i + b) + 3)
                if not first:
                    pe.wait_ge(h["sg_ready"], 2 * i + b)
                if after_rms:
                    pe.wait_ge(h["rstd_ready"], 2 * i + b - 1)
                project(2, piece(wh, 2), piece(wl, 2)).then_inc(h["g_done"], 1)

            def cur_v(i, b, first):
                pe.wait_ge(wh_in[b], i * 64 + 64)
                if not first:
                    pe.wait_ge(h["v_sb"], 2 * i + b)
                for t, (t0, n) in enumerate(TILES):
                    for k in range(KT):
                        last = mm(ps[0:n, 3, t * P:t * P + P], xT[:, k, t0:t0 + n], sh[:, b, 3, k, :], k == 0, k == KT - 1)
                last.then_inc(h["v_done"], 1)

            def levels(i, b, t, first):
                t0, n = TILES[t]
                if t == 0:
                    pe.wait_ge(h["xr_ready"], 2 * i + b + 1)
                    pe.wait_ge(h["xk_ready"], 2 * i + b + 1)
                if not (first and t == 0):
                    pe.wait_ge(h["am_ready"], 3 * (2 * i + b) + t)
                for lv in range(8):
                    if t == 2 and lv == 0:
                        continue
                    lo = ro = None
                    if lv < 7:
                        at = XO[lv] + t0
                        lo = ro = X[b][:, at:at + n]
                    else:
                        lo, ro = hk[:, b, t0:t0 + n], hq[:, b, t0:t0 + n]
                    last = mm(ps[0:n, 4 + lv // 4, (lv % 4) * P:(lv % 4) * P + n], lo, ro, True, True)
                last.then_inc(h["a_done"], 1)

            def prev_kT(i, b, first):
                pe.wait_ge(h["kdec_ready"], 2 * i + b + 1)
                if not first:
                    pe.wait_ge(h["so_ready"], 2 * i + b)
                for t, (t0, n) in enumerate(TILES):
                    last = pe.transpose(ps[0:n, 7, t * P:t * P + P], hkde[:, t0:t0 + n], ident)
                last.then_inc(h["kT_done"], 1)

            def prev_states(i, b):
                n1 = 2 * i + b
                pe.wait_ge(h["kT_sb"], n1 + 1)
                pe.wait_ge(h["v_sb"], n1 + 1)
                for t, (t0, n) in enumerate(TILES):
                    last = mm(ps[:, 7, t * P:t * P + P], hkT[0:n, t, :], hV[0:n, t, :], True, True)
                last.then_inc(h["s_done"], 1)

            def prev_out(i, b, first):
                n1 = 2 * i + b
                if not first:
                    pe.wait_ge(h["o_out"], n1 + 1)
                pe.wait_ge(st_in[b], i * 16 + 16)
                pe.wait_ge(h["qeb_ready"], n1 + 1)
                pe.wait_ge(h["sa_sb"], n1 + 1)
                pe.wait_ge(h["as_ready"], 3 * n1 + 2)
                mm(ps[:, 6, 0:128], hV[:, 0, :], hAS[:, 0, :], True, True)
                mm(ps[:, 6, 128:256], hSA, hqeb[:, 128:256], True, False)
                mm(ps[:, 6, 128:256], hV[:, 1, :], hAS[:, 1, :], False, True)
                mm(ps[:, 6, 256:320], hSst[:, b, :], hqeb[:, 256:320], True, False)
                pe.wait_ge(h["as_ready"], 3 * n1 + 3)
                mm(ps[:, 6, 256:320], hV[0:64, 2, :], hAS[0:64, 2, 0:64], False, True).then_inc(h["o_done"], 1)

            def rms(i, b):
                n1 = 2 * i + b
                pe.wait_ge(h["sg_ready"], n1 + 2)
                pe.wait_ge(h["osq_ready"], n1 + 1)
                mm(ps[:, 2, 0:T], ones, hosq, True, True).then_inc(h["rms_done"], 1)

            def head_turn(cur, prev, pprev, first=False, first_prev=False):
                if cur:
                    cur_f(*cur, first)
                if pprev:
                    rms(*pprev)
                if prev:
                    levels(*prev, 0, first_prev)
                if cur:
                    cur_q(*cur, first)
                if prev:
                    levels(*prev, 1, first_prev)
                    prev_kT(*prev, first_prev)
                if cur:
                    cur_g(*cur, first, pprev is not None)
                if prev:
                    levels(*prev, 2, first_prev)
                    prev_states(*prev)
                if cur:
                    cur_v(*cur, first)
                if prev:
                    prev_out(*prev, first_prev)

            head_turn((0, 0), None, None, first=True)
            head_turn((0, 1), (0, 0), None, first_prev=True)
            with pe.Fori(1, 4) as i:
                head_turn((i, 0), (i - 1, 1), (i - 1, 0))
                head_turn((i, 1), (i, 0), (i - 1, 1))

            def conv_value(c):
                pe.wait_ge(ulo_ready, 2 * c + 1)
                project(U_BANKS[c][0], u_hi[c % 2][0][1], u_lo[c % 2][0][1])

            def conv_gate(c):
                pe.wait_ge(ulo_ready, 2 * c + 2)
                project(U_BANKS[c][1], u_hi[c % 2][1][1], u_lo[c % 2][1][1]).then_inc(u_done, 1)

            rms(3, 0)
            levels(3, 1, 0, False)
            levels(3, 1, 1, False)
            prev_kT(3, 1, False)
            levels(3, 1, 2, False)
            prev_states(3, 1)
            pe.wait_ge(h["rstd_ready"], 7)
            pe.wait_ge(h["sg_ready"], 8)
            pe.wait_ge(h["v_sb"], 8)
            conv_value(0)
            prev_out(3, 1, False)
            conv_gate(0)
            pe.wait_ge(h["osq_ready"], 8)
            pe.wait_ge(h["am_ready"], 24)
            mm(ps[:, 4, 0:T], ones, hosq, True, True).then_inc(h["rms_done"], 1)
            conv_value(1)
            conv_gate(1)
            pe.wait_ge(h["so_ready"], 8)
            conv_value(2)
            conv_gate(2)
            pe.wait_ge(u_ready, 1)
            conv_value(3)
            conv_gate(3)
            pe.wait_ge(h["o_out"], 9)

            def tail(i, b, first):
                if not first:
                    pe.wait_ge(m_ready, 2 * i + b - 1)
                for s in range(2):
                    pe.wait_ge(tlo_ready, 4 * i + 2 * b + s + 1)
                    project(3 * b + s, t_hi[1 - b][s][1], t_lo[1 - b][s][1])
                pe.wait_ge(wt_in[b], i * 16 + 16)
                for k in range(KT):
                    last = mm(ps[:, 3 * b + 2, 0:T], stl[:, b, 16 + k, :], oT[:, k, :], k == 0, k == KT - 1)
                last.then_inc(t_done, 1)

            pe.wait_ge(u_ready, 4)
            tail(0, 0, True)
            tail(0, 1, True)
            with pe.Fori(1, 3) as i:
                tail(i, 0, False)
                tail(i, 1, False)

            pe.wait_ge(conv_done, 4)
            for c in range(CT):
                last = mm(ps[:, 6, 0:CW], ones, cT[:, c, :], c == 0, c == CT - 1)
            last.then_inc(cmean_done, 1)
            tail(3, 0, False)
            pe.wait_ge(csq_ready, 1)
            for c in range(CT):
                last = mm(ps[:, 7, 0:CW], ones, csq[:, c, :], c == 0, c == CT - 1)
            last.then_inc(cvar_done, 1)
            tail(3, 1, False)
            pe.wait_ge(crs_ready, 1)
            for s in range(2):
                for c in range(CT):
                    last = pe.transpose(ps[0:HALO, 6 + s, c * P:c * P + P], utail[:, c, s, :], ident)
            last.then_inc(tailT_done, 1)
            pe.wait_ge(m_ready, 7)
            pe.wait_ge(cn_ready, 8)
            pe.wait_ge(wb_in, 64)
            for d in range(KT):
                if d == 2:
                    pe.wait_ge(m_ready, 8)
                if d >= 4:
                    pe.wait_ge(mb_ready, d - 3)
                for k in range(CT):
                    last = mm(ps[:, (1, 2, 4, 5)[d % 4], 0:T], sob[k][:, d * P:d * P + P], cn[:, k, :], k == 0, k == CT - 1)
                last.then_inc(yb_done, 1)

            pe.wait_ge(mb_ready, 8)
            pe.wait_ge(wo_in, 16)
            for b in range(2):
                for t, (t0, n) in enumerate(TILES):
                    for k in range(4 * b, 4 * b + 4):
                        for hf in range(2):
                            last = mm(ps[0:n, 2 * t + hf, :], mT[:, k, t0:t0 + n], so[:, k, hf * 512:hf * 512 + 512], k == 0, k == KT - 1)
                        if k == 0:
                            for kk in range(KT):
                                mm(ps[0:n, 2 * t + kk // 4, (kk % 4) * P:(kk % 4) * P + P], xT[:, kk, t0:t0 + n], alI, False, False)
                    if b == 1:
                        last.then_inc(mix_done, 1)

            to_features(x1, x1_ready, x1T_done, x1T_sb, X1_BANKS)
            pe.wait_ge(x1T_sb, 6)
            pe.wait_ge(wrt_in, 16)
            for t, (t0, n) in enumerate(TILES):
                for k in range(KT):
                    last = mm(ps[0:n, 4, t * NE:t * NE + NE], x1T[:, k, t0:t0 + n], wrt[:, k, :], k == 0, k == KT - 1)
            last.then_inc(logit_done, 1)
            pe.wait_ge(chosen, 1)
            for t in range(3):
                for s in range(t + 1):
                    last = mm(ps[:, 5, t * NE:t * NE + NE], tri if s == t else ones, rt[:, 1, s, :], s == 0, s == t)
            for s in range(3):
                last = mm(ps[:, 5, 3 * NE:4 * NE], ones, rt[:, 1, s, :], s == 0, s == 2)
            last.then_inc(pos_done, 1)

            def both(bank, lhs, g):
                for kk in range(4):
                    k = 4 * (g % 2) + kk
                    for hf in range(2):
                        for m in range(2):
                            last = mm(ps[64 * m:64 * m + 64, bank + hf, :], lhs[:, k, 64 * m:64 * m + 64], ring[:, g % RING, m, kk, hf * 512:hf * 512 + 512],
                                      k == 0, k == KT - 1)
                return last

            def group(g, i):
                pe.wait_ge(group_in[g % RING], 32 * (12 // RING) * i + 32 * (g // RING) + 32)

            def expert_pair(i, b, first):
                n = 2 * i + b
                pe.wait_ge(e["pick_ready"], n + 1)
                if not first:
                    pe.wait_ge(e["y_added"], 6 * n)
                for k in range(KT):
                    for t, (_, c) in enumerate(TILES):
                        last = mm(ps[:, 4 + k // 4, (k % 4) * P:(k % 4) * P + P], x1[0:c, t, k * P:k * P + P], ePm[0:c, t, :], t == 0, t == 2)
                last.then_inc(e["eXT_done"], 1)
                pe.wait_ge(e["gpick_ready"], n + 1)
                for t, (_, c) in enumerate(TILES):
                    last = pe.transpose(ps[:, 6, t * P:t * P + c], eGm[0:c, t, :], ident[0:c, 0:c])
                last.then_inc(e["eGT_done"], 1)
                pe.wait_ge(e["eXT_a"], n + 1)
                pe.wait_ge(e["eXT_b"], n + 1)
                for g in range(6 * b, 6 * b + 4):
                    group(g, i)
                    both(0 if g < 6 * b + 2 else 2, eXT, g).then_inc(e["group_used"], 1)
                pe.wait_ge(e["eh_ready"], n + 1)
                for k in range(KT):
                    last = pe.transpose(ps[:, 4 + k // 4, (k % 4) * P:(k % 4) * P + P], eh[:, k * P:k * P + P], ident)
                last.then_inc(e["ehT_done"], 1)
                pe.wait_ge(e["ehT_a"], n + 1)
                pe.wait_ge(e["ehT_b"], n + 1)
                pe.wait_ge(e["eGT_sb"], n + 1)
                for g in range(6 * b + 4, 6 * b + 6):
                    group(g, i)
                    both(6, ehT, g).then_inc(e["group_used"], 1)
                pe.wait_ge(e["eos_ready"], n + 1)
                for t, (_, c) in enumerate(TILES):
                    for hf in range(2):
                        j = 2 * t + hf
                        if j >= 4:
                            pe.wait_ge(e["y_added"], 6 * n + j - 3)
                        mm(ps[0:c, 2 + j % 4, :], eGT[:, t, 0:c], eos[:, hf * 512:hf * 512 + 512], True, True).then_inc(e["y_done"], 1)

            expert_pair(0, 0, True)
            expert_pair(0, 1, False)
            with pe.Fori(1, PAIRS // 2) as i:
                expert_pair(i, 0, False)
                expert_pair(i, 1, False)
            more = pe.value_load(flag[0:1, :], min_val=0, max_val=1)
            with pe.If(more != 0):
                with pe.Fori(1, ROUNDS) as r:
                    with pe.Fori(0, PAIRS // 2) as i:
                        expert_pair(PAIRS // 2 * r + i, 0, False)
                        expert_pair(PAIRS // 2 * r + i, 1, False)

        @block.scalar
        def _(act):
            step = Chain(act, act_step)
            act.preload_act_table_set("natural_log_exp_and_others")
            act.wait_ge(setup_done, 1)

            def rstd_of(var, ready, ch):
                for t in range(3):
                    act.wait_ge(var, t + 1)
                    ch(act.activation(rstd3[:, t:t + 1], mv[:, t, 1:2], ACT.Ln, bias=eps1[:, :]))
                    signal(act, act.activation(rstd3[:, t:t + 1], rstd3[:, t:t + 1], ACT.Exp, scale=-0.5), ready, t + 1)

            rstd_of(var0, rstd0, step)

            def copy_features(dst, done, copied, banks, high=None):
                for t, (t0, n) in enumerate(TILES):
                    for hf in range(2):
                        act.wait_ge(done, 2 * t + hf + 1)
                        src = ps[:, banks[2 * t + hf], :].rearrange("p (k n) -> p k n", k=4)[:, :, 0:n]
                        if high is not None:
                            signal(act, act.activation(high[:, 4 * hf:4 * hf + 4, t0:t0 + n], src, ACT.Copy), xh_ready, 2 * t + hf + 1)
                        signal(act, act.activation(dst[:, 4 * hf:4 * hf + 4, t0:t0 + n], src, ACT.Copy), copied, 2 * t + hf + 1)

            copy_features(xT, x0T_done, x0T_sb, X0_BANKS, xhk)

            cc = Chain(act, h["hc_act"], 6)
            pc = Chain(act, h["hp_act"], 1)

            def w_high(i, b, q, first=False):
                n = 2 * i + b
                act.wait_ge(wh_in[b], i * 64 + 64)
                if not first:
                    act.wait_ge(h[("f_done", "q_done", "g_done")[q]], n)
                signal(act, act.activation(piece(wh, q), sh[:, b, q].rearrange("p k n -> p (k n)"), ACT.Copy), whi_ready, 3 * n + q + 1)

            def u_high(c):
                act.wait_ge(wu_in[c], 32)
                if c >= 2:
                    act.wait_ge(u_done, c - 1)
                elif c == 0:
                    act.wait_ge(h["q_done"], 8)
                else:
                    act.wait_ge(h["a_done"], 21)
                for q in range(2):
                    signal(act, act.activation(u_hi[c % 2][q][1], su[:, c, q].rearrange("p k n -> p (k n)"), ACT.Copy), uhi_ready, 2 * c + q + 1)

            def t_high(i, b, first=False):
                n = 2 * i + b
                act.wait_ge(wg_in[b], i * 32 + 32)
                if not first:
                    act.wait_ge(t_done, n - 1)
                    act.dma_start(stl[:, b, 16:24], w_oa_k[:, :, bass.ds(n * P, P)]).then_inc(wt_in[b], 16)
                for q in range(2):
                    signal(act, act.activation(t_hi[1 - b][q][1], stl[:, b, 8 * q:8 * q + 8].rearrange("p k n -> p (k n)"), ACT.Copy), thi_ready, 2 * n + q + 1)

            for q in range(3):
                w_high(0, 0, q, True)
            act.wait_ge(params_ready, 1)

            def forget(i, b, first):
                n = 2 * i + b
                cc.turn(n)
                act.wait_ge(h["f_done"], n + 1)
                if not (first and b == 0):
                    act.wait_ge(h["ls_ready"], n)
                cc(act.activation(he, ps[:, 0, 0:T], ACT.Abs))
                if not (first and b == 0):
                    act.wait_ge(h["b_ready"], n)
                cc(act.activation(hw, ps[:, 0, 0:T], ACT.Exp, scale=-1.0))
                cc(act.activation(he, he, ACT.Exp, scale=-1.0))
                signal(act, act.activation(he, he, ACT.Ln, bias=one1[:, :]), h["e_ready"], n + 1)
                signal(act, act.activation(hw, hw, ACT.Ln, scale=lb[:, bass.ds(n, 1)], bias=one1[:, :]), h["w_ready"], n + 1)

            def q_copy(i, b, first):
                n = 2 * i + b
                act.wait_ge(h["q_done"], n + 1)
                if not first:
                    act.wait_ge(h["a_done"], 3 * n - 3)
                    act.wait_ge(h["qeb_ready"], n - 1)
                signal(act, act.activation(hq[:, b, :], ps[:, 1, 0:T], ACT.Copy, scale=QSCALE), h["q_sb"], n + 1)

            def key_exp(i, b):
                n = 2 * i + b
                act.wait_ge(h["ls_ready"], n + 1)
                signal(act, act.activation(hk[:, b, :], hk[:, b, :], ACT.Exp), h["kexp_ready"], n + 1)

            def g_exp(i, b):
                n = 2 * i + b
                act.wait_ge(h["gc_ready"], n + 1)
                cc(act.activation(hgx, hgx, ACT.Exp, scale=-1.0))
                cc(act.activation(hgx, hgx, ACT.Ln, bias=one1[:, :]))
                signal(act, act.activation(hgx, hgx, ACT.Exp, scale=-1.0), h["gx_ready"], n + 1)

            def v_copy(i, b, first):
                n = 2 * i + b
                act.wait_ge(h["v_done"], n + 1)
                if not first:
                    act.wait_ge(h["o_done"], n)
                cc(act.activation(hV[:, 0:2, :], ps[:, 3, 0:256].rearrange("p (t n) -> p t n", t=2), ACT.Copy))
                signal(act, act.activation(hV[0:64, 2, :], ps[0:64, 3, 256:384], ACT.Copy), h["v_sb"], n + 1)

            def level_exp(i, b):
                n = 2 * i + b
                act.wait_ge(h["dr_ready"], n + 1)
                act.wait_ge(h["dl_ready"], n + 1)
                signal(act, act.activation(X[b], X[b], ACT.Exp), h["E_ready"], n + 1)

            def tile_exp(i, b, first):
                n = 2 * i + b
                if not first:
                    act.wait_ge(h["qeb_ready"], n)
                    act.wait_ge(h["kT_done"], n)
                signal(act, act.activation(heb, hb, ACT.Exp), h["eb_ready"], n + 1)
                for t, (t0, c) in enumerate(TILES):
                    last = act.activation(hkde[:, t0:t0 + c], hb[:, t0:t0 + c], ACT.Exp, scale=-1.0, bias=hb[:, t0 + c - 1:t0 + c])
                    signal(act, last, h["kde_ready"], 3 * n + t + 1)

            def prev_states(i, b, first):
                n = 2 * i + b
                act.wait_ge(h["kT_done"], n + 1)
                if not first:
                    act.wait_ge(h["s_done"], n)
                pc.turn(n)
                pc(act.activation(hkT[:, 0:2, :], ps[:, 7, 0:256].rearrange("p (t n) -> p t n", t=2), ACT.Copy))
                signal(act, act.activation(hkT[0:64, 2, :], ps[0:64, 7, 256:384], ACT.Copy), h["kT_sb"], n + 1)

            def prev_sa(i, b, first):
                n = 2 * i + b
                act.wait_ge(h["s_done"], n + 1)
                if not first:
                    act.wait_ge(h["so_ready"], n)
                    act.wait_ge(h["o_done"], n)
                signal(act, act.activation(hSA, ps[:, 7, 0:P], ACT.Copy), h["sa_sb"], n + 1)

            def prev_square(i, b, first):
                n = 2 * i + b
                act.wait_ge(h["o_done"], n + 1)
                if not first:
                    act.wait_ge(h["rms_done"], n)
                signal(act, act.activation(hosq, ps[:, 6, 0:T], ACT.Square), h["osq_ready"], n + 1)

            def store_states(i, b):
                n = 2 * i + b
                act.wait_ge(h["so_ready"], n + 1)
                for s, name in enumerate(("new_hgrn_prompt", "new_hgrn_sample")):
                    act.dma_start(o[name][0, 0, bass.ds(n, 1)].rearrange("o p n -> (o p) n"), hSo[:, s, :]).then_inc(h["so_stored"], 16)

            def pprev_rms(i, b, bank=2):
                n = 2 * i + b
                act.wait_ge(h["rms_done"], n + 1)
                act.wait_ge(h["o_out"], n + 1)
                signal(act, act.activation(hrs, ps[:, bank, 0:T], ACT.Ln, bias=eps1[:, :], scale=1.0 / P), h["rstd_ready"], n + 1)
                signal(act, act.activation(hrs, hrs, ACT.Exp, scale=-0.5), h["rstd_exp"], n + 1)

            def head_turn(cur, nxt, prev, pprev, first=False, first_prev=False):
                forget(*cur, first or first_prev)
                if pprev:
                    pprev_rms(*pprev)
                key_exp(*cur)
                q_copy(*cur, first or first_prev)
                if nxt:
                    w_high(*nxt, 0)
                if prev:
                    prev_states(*prev, first_prev)
                level_exp(*cur)
                tile_exp(*cur, first)
                if nxt:
                    w_high(*nxt, 1)
                else:
                    u_high(0)
                if prev:
                    prev_sa(*prev, first_prev)
                g_exp(*cur)
                if nxt:
                    w_high(*nxt, 2)
                else:
                    u_high(1)
                if prev:
                    prev_square(*prev, first_prev)
                    store_states(*prev)
                v_copy(*cur, first)

            head_turn((0, 0), (0, 1), None, None, first=True)
            head_turn((0, 1), (1, 0), (0, 0), None, first_prev=True)
            with act.Fori(1, 3) as i:
                head_turn((i, 0), (i, 1), (i - 1, 1), (i - 1, 0))
                head_turn((i, 1), (i + 1, 0), (i, 0), (i - 1, 1))
            head_turn((3, 0), (3, 1), (2, 1), (2, 0))
            head_turn((3, 1), None, (3, 0), (2, 1))
            pprev_rms(3, 0)
            prev_states(3, 1, False)
            prev_sa(3, 1, False)

            def conv_gate(i, b):
                n = 2 * i + b
                act.wait_ge(u_done, n + 1)
                if i:
                    act.wait_ge(u_ready, b + 1)
                signal(act, act.activation(sgu[:, b, :], ps[:, U_BANKS[n][1], 0:T], ACT.Sigmoid), sgu_ready, n + 1)

            prev_square(3, 1, False)
            store_states(3, 1)
            conv_gate(0, 0)
            u_high(2)
            pprev_rms(3, 1, bank=4)
            conv_gate(0, 1)
            u_high(3)
            t_high(0, 0, True)
            conv_gate(1, 0)
            conv_gate(1, 1)
            act.wait_ge(u_done, 4)
            t_high(0, 1, True)

            def tail(i, b, first=False):
                n = 2 * i + b
                act.wait_ge(t_done, n + 1)
                if not first:
                    act.wait_ge(m_ready, n - 1)
                signal(act, act.activation(sgt[:, b, :], ps[:, 3 * b, 0:T], ACT.Sigmoid), sgt_ready, 2 * n + 1)
                dst = sgb[:, bass.ds(n, 1), :].rearrange("p o n -> p (o n)")
                signal(act, act.activation(dst, ps[:, 3 * b + 1, 0:T], ACT.Sigmoid), sgt_ready, 2 * n + 2)

            t_high(1, 0)
            tail(0, 0, True)
            t_high(1, 1)
            tail(0, 1, True)
            with act.Fori(1, 3) as i:
                t_high(i + 1, 0)
                tail(i, 0)
                t_high(i + 1, 1)
                tail(i, 1)

            act.wait_ge(cdiff_ready, 1)
            act.wait_ge(h["so_stored"], 256)
            signal(act, act.activation(csq, cT, ACT.Square), csq_ready, 1)
            tail(3, 0)
            act.wait_ge(cvar_done, 1)
            step(act.activation(crs, ps[:, 7, 0:CW], ACT.Ln, bias=eps1[:, :], scale=1.0 / DB))
            signal(act, act.activation(crs, crs, ACT.Exp, scale=-0.5), crs_ready, 1)
            act.wait_ge(cz_ready, 1)
            for c in range(CT):
                for s, (dst, src) in enumerate(((slice(0, SEQ), slice(0, SEQ)), (slice(SEQ, T), slice(SEQ + HALO, CW)))):
                    signal(act, act.activation(cn[:, c, dst], cT[:, c, src], ACT.Silu, scale=vt[:, c, 32:33], bias=vt[:, c, 33:34]), cn_ready, 2 * c + s + 1)
            tail(3, 1)
            act.wait_ge(tailT_done, 1)
            for s in range(2):
                signal(act, act.activation(ncv[0:HALO, s, :], ps[0:HALO, 6 + s, :], ACT.Copy), tail_sb, s + 1)
                act.dma_start(o[("new_conv_prompt", "new_conv_sample")[s]][0, 0], ncv[0:HALO, s, :]).then_inc(tail_stored, 16)
            act.preload_act_table_set("natural_log_exp_and_others")

            rstd_of(var1, rstd1, step)
            copy_features(x1T, x1T_done, x1T_sb, X1_BANKS)
            act.wait_ge(lmax_ready, 1)
            signal(act, act.activation(L16, L16, ACT.Exp), lexp_ready, 1)
            act.wait_ge(x1_ready, 3)
            for t, (_, n) in enumerate(TILES):
                signal(act, act.activation(yacc[0:n, t, :], x1[0:n, t, :], ACT.Copy, scale=ALPHA), yacc_ready, t + 1)

            def expert_pair(n, first):
                act.wait_ge(e["eXT_done"], n + 1)
                signal(act, act.activation(eXT[:, 0:4, :], ps[:, 4, :].rearrange("p (k n) -> p k n", k=4), ACT.Copy), e["eXT_a"], n + 1)
                act.wait_ge(e["eGT_done"], n + 1)
                signal(act, act.activation(eGT[:, :, :].rearrange("p t n -> p (t n)")[:, 0:T], ps[:, 6, 0:T], ACT.Copy), e["eGT_sb"], n + 1)
                act.wait_ge(e["group_used"], 6 * n + 2)
                signal(act, act.activation(ehs, ps[:, 0:2, :].rearrange("p b n -> p (b n)"), ACT.Silu), e["silu_ready"], n + 1)
                act.wait_ge(e["ehT_done"], n + 1)
                signal(act, act.activation(ehT[:, 0:4, :], ps[:, 4, :].rearrange("p (k n) -> p k n", k=4), ACT.Copy), e["ehT_a"], n + 1)
                act.wait_ge(e["group_used"], 6 * n + 6)
                signal(act, act.activation(eos, ps[:, 6:8, :].rearrange("p b n -> p (b n)"), ACT.Copy), e["eos_ready"], n + 1)

            with act.Fori(0, PAIRS) as p:
                expert_pair(p, False)
            more = act.value_load(flag[0:1, :], min_val=0, max_val=1)
            with act.If(more != 0):
                with act.Fori(1, ROUNDS) as r:
                    with act.Fori(0, PAIRS) as p:
                        expert_pair(PAIRS * r + p, False)
            rstd_of(var2, rstd2, step)
            act.wait_ge(tail_stored, 32)
            act.wait_ge(h["so_stored"], 256)
            for t, (t0, c) in enumerate(TILES):
                act.wait_ge(y_ready, t + 1)
                dst = o["y_prompt"][0, t0:t0 + c] if t < 2 else o["y_sample"][0]
                act.dma_start(dst, yacc[0:c, t, :]).then_inc(y_stored, 16)
            act.wait_ge(y_stored, 48)

        @block.gpsimd
        def _(pool):
            cc = Chain(pool, h["hc_pool"], 12)
            pc = Chain(pool, h["hp_pool"], 6)

            def key_decay(i, b):
                n = 2 * i + b
                cc.turn(n)
                pool.wait_ge(h["b_ready"], n + 1)
                for lv, hs in enumerate(LV):
                    w = SEQ if lv == 0 else T
                    xv = X[b][:, XO[lv]:XO[lv] + w].rearrange("p (m s) -> p m s", s=2 * hs)[:, :, 0:hs]
                    bv = hb[:, 0:w].rearrange("p (m s) -> p m s", s=2 * hs)
                    ins = pool.tensor_tensor(xv, bv[:, :, hs - 1:hs].to_broadcast([P, w // (2 * hs), hs]), bv[:, :, 0:hs], ALU.subtract)
                    if lv < 6:
                        cc(ins)
                signal(pool, ins, h["dl_ready"], n + 1)

            def key_side(i, b):
                n = 2 * i + b
                pool.wait_ge(h["E_ready"], n + 1)
                pool.wait_ge(h["k_ready"], n + 1)
                for lv, hs in enumerate(LV):
                    w = SEQ if lv == 0 else T
                    xv = X[b][:, XO[lv]:XO[lv] + w].rearrange("p (m s) -> p m s", s=2 * hs)[:, :, 0:hs]
                    kv = hk[:, b, 0:w].rearrange("p (m s) -> p m s", s=2 * hs)[:, :, 0:hs]
                    ins = pool.tensor_tensor(xv, xv, kv, ALU.mult)
                    if lv < 6:
                        cc(ins)
                signal(pool, ins, h["xk_ready"], n + 1)
                cc.end()

            def level_sums(i, b, tiles, first):
                n = 2 * i + b
                if tiles[0] == 0:
                    pc.turn(n)
                for t in tiles:
                    w = TILES[t][1]
                    pool.wait_ge(h["am_ready"], 3 * n + t + 1)
                    am = hAM[(b + t) % 2][0:w]
                    if t == 0 and not first:
                        pool.wait_ge(h["o_done"], n)
                    lo = 0 if t < 2 else 1
                    left = 4 if t < 2 else 3
                    pc(pool.tensor_tensor(am[:, lo:lo + left, 0:w], am[:, lo:lo + left, 0:w], am[:, lo + 4:lo + 4 + left, 0:w], ALU.add))
                    rest = 2
                    pc(pool.tensor_tensor(am[:, lo:lo + rest, 0:w], am[:, lo:lo + rest, 0:w], am[:, lo + 2:lo + 2 + rest, 0:w], ALU.add))
                    signal(pool, pool.tensor_tensor(hAS[0:w, t, 0:w], am[:, lo, 0:w], am[:, lo + 1, 0:w], ALU.add), h["as_ready"], 3 * n + t + 1)
                if tiles[-1] == 2:
                    pc.end()

            def head_turn(cur, prev, first_prev=False):
                if prev:
                    level_sums(*prev, [0], first_prev)
                if cur:
                    key_decay(*cur)
                if prev:
                    level_sums(*prev, [1], first_prev)
                    level_sums(*prev, [2], first_prev)
                if cur:
                    key_side(*cur)

            head_turn((0, 0), None)
            head_turn((0, 1), (0, 0), True)
            with pool.Fori(1, 4) as i:
                head_turn((i, 0), (i - 1, 1))
                head_turn((i, 1), (i, 0))

            def u_low(c):
                for q in range(2):
                    pool.wait_ge(uhi_ready, 2 * c + q + 1)
                    signal(pool, pool.tensor_tensor(u_lo[c % 2][q][1], su[:, c, q].rearrange("p k n -> p (k n)"), u_hi[c % 2][q][0], ALU.subtract), ulo_ready, 2 * c + q + 1)

            def t_low(i, b):
                n = 2 * i + b
                for q in range(2):
                    pool.wait_ge(thi_ready, 2 * n + q + 1)
                    signal(pool, pool.tensor_tensor(t_lo[1 - b][q][1], stl[:, b, 8 * q:8 * q + 8].rearrange("p k n -> p (k n)"), t_hi[1 - b][q][0], ALU.subtract),
                           tlo_ready, 2 * n + q + 1)

            u_low(0)
            head_turn(None, (3, 1))
            for c in range(1, CT):
                u_low(c)
            with pool.Fori(0, 4) as i:
                t_low(i, 0)
                t_low(i, 1)

        @block.vector
        def _(dve):
            step = Chain(dve, dve_step)
            step(dve.memset(one1[:, :], 1.0))
            step(dve.memset(eps1[:, :], EPS))
            step(dve.memset(mv[:, :, :], 1.0))
            step(dve.memset(ones, 1.0))
            signal(dve, dve.memset(uc[:, :, 0:HALO], 0.0), setup_done, 1)

            def norm_stats(halves, t, n, ch):
                for hf in range(2):
                    ch(dve.bn_stats(stats[0:n, t, hf, :], halves[hf]))

            def norm_apply(dst, src, t, n, g, b, rstd, ready, ch):
                ch(dve.scalar_tensor_tensor(dst, src, mv[0:n, t, 0:1], g, ALU.subtract, ALU.mult))
                dve.wait_ge(rstd, t + 1)
                signal(dve, dve.scalar_tensor_tensor(dst, dst, rstd3[0:n, t:t + 1], b, ALU.mult, ALU.add), ready, t + 1)

            for t, (_, n) in enumerate(TILES):
                dve.wait_ge(x_in[t], 16)
                norm_stats([x0[0:n, t, 0:512], x0[0:n, t, 512:1024]], t, n, step)
                ins = dve.bn_aggr(mv[0:n, t, :], stats[0:n, t, :, :].rearrange("p s n -> p (s n)"))
                signal(dve, ins, var0, t + 1)
            dve.wait_ge(gb0_in, 32)
            for t, (_, n) in enumerate(TILES):
                norm_apply(x0[0:n, t, :], x0[0:n, t, :], t, n, gb0[0:n, 0, :], gb0[0:n, 1, :], rstd0, x0_ready, step)

            def x_low(j):
                t0, n = TILES[j // 2]
                hf = j % 2
                dve.wait_ge(x0T_sb, j + 1)
                v = lambda m: m[:, 4 * hf:4 * hf + 4, t0:t0 + n]
                signal(dve, dve.tensor_tensor(v(xlk), v(xT), v(xhkF), ALU.subtract), xl_ready, j + 1)

            def w_low(i, b, q):
                n = 2 * i + b
                dve.wait_ge(whi_ready, 3 * n + q + 1)
                signal(dve, dve.tensor_tensor(piece(wl, q), sh[:, b, q].rearrange("p k n -> p (k n)"), piece(whF, q), ALU.subtract), wlo_ready, 3 * n + q + 1)

            for j in range(6):
                x_low(j)
            for q in range(3):
                w_low(0, 0, q)

            dve.wait_ge(mask_in, 16)
            step(dve.tensor_copy(mask[:, :, :].rearrange("p l n -> p (l n)"), maskf))
            dve.wait_ge(rowsT_done, 1)
            step(dve.tensor_copy(vt[:, :, :].rearrange("p c n -> p (c n)"), ps[:, 7, 0:256]))
            step(dve.tensor_copy(hv[:, :], ps[:, 7, 256:265]))
            step(dve.tensor_tensor(lb[:, :], hv[:, 0:8], hv[:, 0:8], ALU.subtract))
            signal(dve, dve.tensor_scalar(olb[:, :], lb[:, :], -1.0, 1.0, ALU.mult, ALU.add), params_ready, 1)

            dve.wait_ge(x0T_done, 6)
            signal(dve, dve.memset(hrs, 0.0), h["o_out"], 1)
            cc = Chain(dve, h["hc_dve"], 15)
            pc = Chain(dve, h["hp_dve"], 1)

            def forget_in(i, b, first):
                n = 2 * i + b
                cc.turn(n)
                dve.wait_ge(h["w_ready"], n + 1)
                cc(dve.scalar_tensor_tensor(hls, ps[:, 0, 0:T], 0.0, he, ALU.min, ALU.subtract))
                if not first:
                    dve.wait_ge(h["a_done"], 3 * n - 3)
                signal(dve, dve.tensor_tensor(hk[:, b, :], hls, ps[:, 0, 0:T], ALU.subtract), h["ls_ready"], n + 1)
                cc(dve.tensor_tensor(hls, hls, hw, ALU.add))
                if not (first and b == 0):
                    dve.wait_ge(h["kde_ready"], 3 * n)
                    dve.wait_ge(h["dl_ready"], n)
                signal(dve, dve.tensor_tensor_scan(hb, reset, hls, 0.0, ALU.mult, ALU.add), h["b_ready"], n + 1)

            def level_decay(i, b):
                n = 2 * i + b
                for lv, hs in enumerate(LV):
                    w = SEQ if lv == 0 else T
                    xv = X[b][:, XO[lv]:XO[lv] + w].rearrange("p (m s) -> p m s", s=2 * hs)
                    bv = hb[:, 0:w].rearrange("p (m s) -> p m s", s=2 * hs)
                    ins = dve.tensor_tensor(xv[:, :, hs:2 * hs], bv[:, :, hs:2 * hs], bv[:, :, hs - 1:hs].to_broadcast([P, w // (2 * hs), hs]), ALU.subtract)
                    if lv < 6:
                        cc(ins)
                signal(dve, ins, h["dr_ready"], n + 1)

            def key_scale(i, b):
                n = 2 * i + b
                dve.wait_ge(h["kexp_ready"], n + 1)
                signal(dve, dve.tensor_scalar(hk[:, b, :], hk[:, b, :], olb[:, bass.ds(n, 1)], None, ALU.mult), h["k_ready"], n + 1)

            def g_clamp(i, b):
                n = 2 * i + b
                dve.wait_ge(h["g_done"], n + 1)
                signal(dve, dve.tensor_scalar(hgx, ps[:, 2, 0:T], -40.0, None, ALU.max), h["gc_ready"], n + 1)

            def g_silu(i, b):
                n = 2 * i + b
                dve.wait_ge(h["gx_ready"], n + 1)
                signal(dve, dve.tensor_tensor(hsg[:, b, :], ps[:, 2, 0:T], hgx, ALU.mult), h["sg_ready"], n + 1)

            def query_side(i, b):
                n = 2 * i + b
                dve.wait_ge(h["E_ready"], n + 1)
                dve.wait_ge(h["q_sb"], n + 1)
                for lv, hs in enumerate(LV):
                    w = SEQ if lv == 0 else T
                    xv = X[b][:, XO[lv]:XO[lv] + w].rearrange("p (m s) -> p m s", s=2 * hs)[:, :, hs:2 * hs]
                    qv = hq[:, b, 0:w].rearrange("p (m s) -> p m s", s=2 * hs)[:, :, hs:2 * hs]
                    ins = dve.tensor_tensor(xv, xv, qv, ALU.mult)
                    if lv < 6:
                        cc(ins)
                signal(dve, ins, h["xr_ready"], n + 1)

            def carry_side(i, b, first):
                n = 2 * i + b
                dve.wait_ge(h["kde_ready"], 3 * n + 3)
                cc(dve.tensor_copy(hebl[:, b, :], heb[:, SEQ - 1:T:DEC]))
                if not first:
                    dve.wait_ge(h["o_done"], n)
                signal(dve, dve.tensor_tensor(hqeb, heb, hq[:, b, :], ALU.mult), h["qeb_ready"], n + 1)
                signal(dve, dve.tensor_tensor(hkde, hkde, hk[:, b, :], ALU.mult), h["kdec_ready"], n + 1)
                cc.end()

            def level_mask(i, b, t, first):
                n = 2 * i + b
                w = TILES[t][1]
                dve.wait_ge(h["a_done"], 3 * n + t + 1)
                if not (first and t < 2):
                    dve.wait_ge(h["as_ready"], 3 * n + t - 1)
                pv = ps[:, 4:6, :].rearrange("p b (l n) -> p (b l) n", l=4)
                lo = 0 if t < 2 else 1
                signal(dve, dve.tensor_tensor(hAM[(b + t) % 2][0:w, lo:8, 0:w], pv[0:w, lo:8, 0:w], mask[0:w, lo:8, 0:w], ALU.mult), h["am_ready"], 3 * n + t + 1)

            def prev_final(i, b, first):
                n = 2 * i + b
                pc.turn(n)
                dve.wait_ge(h["sa_sb"], n + 1)
                if not first:
                    dve.wait_ge(h["so_stored"], 32 * n)
                pc(dve.scalar_tensor_tensor(hSo[:, 0, :], hSA, hebl[:, b, 0:1], ps[:, 7, P:2 * P], ALU.mult, ALU.add))
                dve.wait_ge(st_in[b], i * 16 + 16)
                signal(dve, dve.scalar_tensor_tensor(hSo[:, 1, :], hSst[:, b, :], hebl[:, b, 1:2], ps[:, 7, 2 * P:3 * P], ALU.mult, ALU.add), h["so_ready"], n + 1)
                pc.end()

            oc = Chain(dve, h["ho_dve"], 1)

            def pprev_out(i, b):
                n = 2 * i + b
                oc.turn(n)
                dve.wait_ge(h["rstd_exp"], n + 1)
                oc(dve.scalar_tensor_tensor(hrs, ps[:, 6, 0:T], hv[:, 8:9], hrs, ALU.mult, ALU.mult))
                signal(dve, dve.tensor_tensor(oT[:, bass.ds(n, 1), :].rearrange("p o n -> p (o n)"), hrs, hsg[:, b, :], ALU.mult), h["o_out"], n + 2)

            def head_turn(cur, nxt, prev, pprev, first=False, first_prev=False):
                if prev:
                    level_mask(*prev, 0, first_prev)
                forget_in(*cur, first or first_prev)
                level_decay(*cur)
                if pprev:
                    pprev_out(*pprev)
                key_scale(*cur)
                if prev:
                    level_mask(*prev, 1, first_prev)
                if nxt:
                    w_low(*nxt, 0)
                if prev:
                    level_mask(*prev, 2, first_prev)
                query_side(*cur)
                g_clamp(*cur)
                if nxt:
                    w_low(*nxt, 1)
                if prev:
                    prev_final(*prev, first_prev)
                g_silu(*cur)
                carry_side(*cur, first)
                if nxt:
                    w_low(*nxt, 2)

            head_turn((0, 0), (0, 1), None, None, first=True)
            head_turn((0, 1), (1, 0), (0, 0), None, first_prev=True)
            with dve.Fori(1, 3) as i:
                head_turn((i, 0), (i, 1), (i - 1, 1), (i - 1, 0))
                head_turn((i, 1), (i + 1, 0), (i, 0), (i - 1, 1))
            head_turn((3, 0), (3, 1), (2, 1), (2, 0))
            head_turn((3, 1), None, (3, 0), (2, 1))
            level_mask(3, 1, 0, False)
            pprev_out(3, 0)
            level_mask(3, 1, 1, False)
            level_mask(3, 1, 2, False)
            prev_final(3, 1, False)

            vc = Chain(dve, conv_step)

            def conv_gate(c):
                b = c % 2
                vc(dve.tensor_copy(uc[:, c, HALO + SEQ:2 * HALO + SEQ], vt[:, c, 34:64]))
                dve.wait_ge(sgu_ready, c + 1)
                vc(dve.tensor_tensor(uc[:, c, HALO:HALO + SEQ], ps[:, U_BANKS[c][0], 0:SEQ], sgu[:, b, 0:SEQ], ALU.mult))
                signal(dve, dve.tensor_tensor(uc[:, c, 2 * HALO + SEQ:UW], ps[:, U_BANKS[c][0], SEQ:T], sgu[:, b, SEQ:T], ALU.mult), u_ready, c + 1)

            HALF = TAPS // 2

            def conv_taps_a(c):
                vc(dve.tensor_copy(utail[:, c, 0, :], uc[:, c, SEQ:SEQ + HALO]))
                vc(dve.tensor_copy(utail[:, c, 1, :], uc[:, c, UW - HALO:UW]))
                vc(dve.tensor_scalar(acc, uc[:, c, 0:CW], vt[:, c, 0:1], vt[:, c, 31:32], ALU.mult, ALU.add))
                for j in range(1, HALF):
                    vc(dve.scalar_tensor_tensor(acc, uc[:, c, j:j + CW], vt[:, c, j:j + 1], acc, ALU.mult, ALU.add))

            def conv_taps_b(c):
                for j in range(HALF, TAPS - 1):
                    vc(dve.scalar_tensor_tensor(acc, uc[:, c, j:j + CW], vt[:, c, j:j + 1], acc, ALU.mult, ALU.add))
                signal(dve, dve.scalar_tensor_tensor(cT[:, c, :], uc[:, c, TAPS - 1:TAPS - 1 + CW], vt[:, c, TAPS - 1:TAPS], acc, ALU.mult, ALU.add),
                       conv_done, c + 1)

            def tail(i, b):
                n = 2 * i + b
                dve.wait_ge(sgt_ready, 2 * n + 2)
                signal(dve, dve.tensor_tensor(mT[:, bass.ds(n, 1), :].rearrange("p o n -> p (o n)"), ps[:, 3 * b + 2, 0:T], sgt[:, b, :], ALU.mult), m_ready, n + 1)

            conv_gate(0)
            pprev_out(3, 1)
            conv_taps_a(0)
            conv_gate(1)
            conv_taps_b(0)
            conv_gate(2)
            conv_gate(3)
            for n in range(6):
                (conv_taps_a, conv_taps_b)[n % 2](1 + n // 2)
                tail(n // 2, n % 2)

            dve.wait_ge(cmean_done, 1)
            step(dve.tensor_scalar(crs, ps[:, 6, 0:CW], 1.0 / DB, None, ALU.mult))
            for c in range(CT):
                ins = dve.tensor_tensor(cT[:, c, :], cT[:, c, :], crs, ALU.subtract)
                if c < CT - 1:
                    step(ins)
            signal(dve, ins, cdiff_ready, 1)
            tail(3, 0)
            dve.wait_ge(crs_ready, 1)
            for c in range(CT):
                ins = dve.tensor_tensor(cT[:, c, :], cT[:, c, :], crs, ALU.mult)
                if c < CT - 1:
                    step(ins)
            signal(dve, ins, cz_ready, 1)
            tail(3, 1)
            step(dve.tensor_scalar(alI, ident, ALPHA, None, ALU.mult))

            bc = Chain(dve, mb_step)
            for d in range(KT):
                dve.wait_ge(yb_done, d + 1)
                bc(dve.tensor_tensor(t12[:, d % 2, :], ps[:, (1, 2, 4, 5)[d % 4], 0:T], sgb[:, d, :], ALU.mult))
                signal(dve, dve.tensor_tensor(mT[:, d, :], mT[:, d, :], t12[:, d % 2, :], ALU.add), mb_ready, d + 1)

            def stats1(t, n):
                dve.wait_ge(mix_done, t + 1)
                norm_stats([ps[0:n, 2 * t, :], ps[0:n, 2 * t + 1, :]], t, n, step)
                signal(dve, dve.bn_aggr(mv[0:n, t, :], stats[0:n, t, :, :].rearrange("p s n -> p (s n)")), var1, t + 1)

            def apply1(t, n):
                norm_apply(x1[0:n, t, :], ps[0:n, 2 * t:2 * t + 2, :].rearrange("p b n -> p (b n)"), t, n, gb1[0:n, 0, :], gb1[0:n, 1, :], rstd1, x1_ready, step)

            dve.wait_ge(gb1_in, 32)
            stats1(0, 128)
            apply1(0, 128)
            stats1(1, 128)
            apply1(1, 128)
            stats1(2, 64)
            apply1(2, 64)

            rs = Chain(dve, route_step)
            rs(dve.memset(L16, 0.0))
            dve.wait_ge(logit_done, 1)
            for t, (_, n) in enumerate(TILES):
                rs(dve.tensor_copy(L16[0:n, t, :], ps[0:n, 4, t * NE:t * NE + NE]))
            mx = cnt[:, 0:3]
            w3 = [P, 3, NE]

            def b3(v):
                return v.rearrange("p (t o) -> p t o", o=1).to_broadcast(w3)

            def bi(v):
                return v.rearrange("p (o n) -> p o n", o=1).to_broadcast(w3)

            rs(dve.tensor_reduce(mx, L16, AX_X, ALU.max))
            signal(dve, dve.tensor_tensor(L16, L16, b3(mx), ALU.subtract), lmax_ready, 1)
            dve.wait_ge(lexp_ready, 1)
            rs(dve.tensor_reduce(mx, L16, AX_X, ALU.add))
            rs(dve.reciprocal(mx, mx))
            rs(dve.tensor_tensor(S16, L16, b3(mx), ALU.mult))
            dve.wait_ge(rb_in, 16)
            rs(dve.tensor_tensor(Z16, S16, bi(rb), ALU.add))
            zg = Z16.rearrange("p t (g s) -> p (t g) s", g=GR)
            rs(dve.tensor_tensor(PS6[:, :, 0:3], zg[:, :, 0:3], zg[:, :, 1:4], ALU.add))
            rs(dve.tensor_tensor(PS6[:, :, 3:5], zg[:, :, 0:2], zg[:, :, 2:4], ALU.add))
            rs(dve.tensor_tensor(PS6[:, :, 5:6], zg[:, :, 0:1], zg[:, :, 3:4], ALU.add))
            gsc, gone = G3[:, 0:3, :], G3[:, 3:6, :]
            rs(dve.tensor_reduce(gsc.rearrange("p t g -> p (t g)"), PS6, AX_X, ALU.max))

            def first_best(score, one, idx, n, work):
                wide = [P, 3, n]
                bb = lambda v: v.rearrange("p (t o) -> p t o", o=1).to_broadcast(wide)
                ib = idx.rearrange("p (o n) -> p o n", o=1).to_broadcast(wide)
                rs(dve.tensor_reduce(mx, score, AX_X, ALU.max))
                rs(dve.tensor_tensor(one, score, bb(mx), ALU.is_equal))
                rs(dve.tensor_scalar(work, one, -1.0e3, 1.0e3, ALU.mult, ALU.add))
                rs(dve.tensor_tensor(work, work, ib, ALU.add))
                rs(dve.tensor_reduce(mx, work, AX_X, ALU.min))
                rs(dve.tensor_tensor(one, work, bb(mx), ALU.is_equal))

            first_best(gsc, gone, i4, GR, G4[:, 0:3, :])
            def by_group(v):
                return v.rearrange("p t (g o) -> p (t g) o", o=1).to_broadcast([P, 3 * GR, NE // GR])

            mg = M16.rearrange("p t (g s) -> p (t g) s", g=GR)
            rs(dve.tensor_tensor(mg, zg, by_group(gone), ALU.mult))
            rs(dve.tensor_scalar(G4[:, 0:3, :], gone, -MASK_SCORE, MASK_SCORE, ALU.mult, ALU.add))
            rs(dve.tensor_tensor(mg, mg, by_group(G4[:, 0:3, :]), ALU.add))
            first_best(M16, O1, i16, NE, N16)
            rs(dve.scalar_tensor_tensor(M16, O1, -1.0e9, M16, ALU.mult, ALU.add))
            first_best(M16, O2, i16, NE, N16)
            rs(dve.tensor_tensor(O1, O1, O2, ALU.add))
            rs(dve.tensor_tensor(GT16, O1, S16, ALU.mult))
            rs(dve.tensor_reduce(mx, GT16, AX_X, ALU.add))
            rs(dve.reciprocal(mx, mx))
            rs(dve.tensor_tensor(rt[:, 2], GT16, b3(mx), ALU.mult))
            rs(dve.memset(O1[64:128, 2, :], 0.0))
            rs(dve.memset(rt[64:128, 2, 2, :], 0.0))
            signal(dve, dve.tensor_copy(rt[:, 1], O1), chosen, 1)
            dve.wait_ge(pos_done, 1)
            rs(dve.tensor_copy(rt[:, 0], ps[:, 5, 0:3 * NE].rearrange("p (t n) -> p t n", t=3)))
            rs(dve.tensor_reduce(cnt[:, 4:5], ps[:, 5, 3 * NE:4 * NE], AX_X, ALU.max))
            rs(dve.tensor_scalar(cnt[:, 5:6], cnt[:, 4:5], float(CAP), None, ALU.is_gt))
            signal(dve, dve.tensor_copy(flag, cnt[:, 5:6]), routed, 1)

            ec = Chain(dve, e["e_dve"], 11)

            def picks(n, p):
                ec.turn(n)
                ec(dve.tensor_copy(cur, rt[:, :, :, bass.ds(2 * p, 2)]))
                for t in range(3):
                    for m in range(2):
                        pick = ec if (t, m) != (2, 1) else lambda ins: signal(dve, ins, e["pick_ready"], n + 1)
                        pick(dve.tensor_scalar(ePm[:, t, 64 * m:64 * m + 64], i64, cur[:, 0, t, m:m + 1], cur[:, 1, t, m:m + 1], ALU.is_equal, ALU.mult))
                for t in range(3):
                    for m in range(2):
                        ins = dve.tensor_scalar(eGm[:, t, 64 * m:64 * m + 64], i64, cur[:, 0, t, m:m + 1], cur[:, 2, t, m:m + 1], ALU.is_equal, ALU.mult)
                        if (t, m) != (2, 1):
                            ec(ins)
                signal(dve, ins, e["gpick_ready"], n + 1)
                ec.end()

            def expert_pair(n, p):
                picks(n, p)
                dve.wait_ge(e["eXT_done"], n + 1)
                signal(dve, dve.tensor_copy(eXT[:, 4:8, :], ps[:, 5, :].rearrange("p (k n) -> p k n", k=4)), e["eXT_b"], n + 1)
                dve.wait_ge(e["group_used"], 6 * n + 4)
                dve.wait_ge(e["silu_ready"], n + 1)
                signal(dve, dve.tensor_tensor(eh, ehs, ps[:, 2:4, :].rearrange("p b n -> p (b n)"), ALU.mult), e["eh_ready"], n + 1)
                dve.wait_ge(e["ehT_done"], n + 1)
                signal(dve, dve.tensor_copy(ehT[:, 4:8, :], ps[:, 5, :].rearrange("p (k n) -> p k n", k=4)), e["ehT_b"], n + 1)
                for t, (_, c) in enumerate(TILES):
                    for hf in range(2):
                        j = 2 * t + hf
                        dve.wait_ge(e["y_done"], 6 * n + j + 1)
                        yv = yacc[0:c, t, hf * 512:hf * 512 + 512]
                        signal(dve, dve.tensor_tensor(yv, yv, ps[0:c, 2 + j % 4, :], ALU.add), e["y_added"], 6 * n + j + 1)

            dve.wait_ge(yacc_ready, 3)
            dve.wait_ge(tail_stored, 32)
            with dve.Fori(0, PAIRS) as p:
                expert_pair(p, p)
            more = dve.value_load(flag[0:1, :], min_val=0, max_val=1)
            with dve.If(more != 0):
                with dve.Fori(1, ROUNDS) as r:
                    dve.tensor_scalar(rt[:, 0], rt[:, 0], float(-CAP), None, ALU.add).then_inc(h["round"], 1)
                    with dve.Fori(0, PAIRS) as p:
                        dve.wait_ge(h["round"], r)
                        expert_pair(PAIRS * r + p, p)

            ns = Chain(dve, norm_step)

            def stats2(t, n):
                norm_stats([yacc[0:n, t, 0:512], yacc[0:n, t, 512:1024]], t, n, ns)
                signal(dve, dve.bn_aggr(mv[0:n, t, :], stats[0:n, t, :, :].rearrange("p s n -> p (s n)")), var2, t + 1)

            def apply2(t, n):
                norm_apply(yacc[0:n, t, :], yacc[0:n, t, :], t, n, g2[0:n, :], b2[0:n, :], rstd2, y_ready, ns)

            dve.wait_ge(gb2_in, 32)
            stats2(0, 128)
            apply2(0, 128)
            stats2(1, 128)
            apply2(1, 128)
            stats2(2, 64)
            apply2(2, 64)


_INS = ["x_prompt", "x_sample", "state_hgrn", "state_conv", "ln_in_g", "ln_in_b", "w_in", "lb_logits", "hg_norm_g", "w_o_a",
        "conv_w", "conv_b", "cn_g", "cn_b", "w_o_b", "w_out", "ln1_g", "ln1_b", "w_router", "router_bias", "w_gate_e",
        "w_up_e", "w_down_e", "ln2_g", "ln2_b"]
_OUTS = [("y_prompt", (1, SEQ, D)), ("y_sample", (1, DEC, D)), ("new_hgrn_prompt", (1, 1, HEADS, P, P)), ("new_conv_prompt", (1, 1, HALO, DB)),
         ("new_hgrn_sample", (1, 1, HEADS, P, P)), ("new_conv_sample", (1, 1, HALO, DB))]


def kernel(**inputs):
    import numpy as _np
    import concourse.bacc as _bacc
    from concourse.bass_utils import run_bass_kernel_spmd as _run

    nc = _bacc.Bacc("TRN2", target_bir_lowering=False, num_devices=1)
    arrays, a, o = {}, {}, {}
    given = {n: _np.ascontiguousarray(inputs[n]) for n in _INS}
    given["consts"], given["masks"] = shape_constants()
    for name, v in given.items():
        arrays[f"in_{name}"] = v
        a[name] = nc.dram_tensor(f"in_{name}", v.shape, mybir.dt.from_np(v.dtype), kind="ExternalInput").ap()
    for name, shape in _OUTS:
        o[name] = nc.dram_tensor(f"out_{name}", shape, F32, kind="ExternalOutput").ap()
    build(nc, a, o)
    r = _run(nc, [arrays], core_ids=[0])
    return tuple(r.results[0][f"out_{name}"] for name, _ in _OUTS)
```
